# Optimizing a Trainium2 kernel written in Bass

```python
import jax
import jax.numpy as jnp
from jax import lax
import numpy as np

D_MODEL = 1024
BATCH = 1
SEQ = 128
DEPTH = 1
DEC_BATCH = 1
DEC_SEQ = 1024
PAST_LEN = 128

GRID_W = 64
D_MIX = D_MODEL
HEAD_DIM = 64
ATTN_WIDTH = D_MIX // 2
HYENA_WIDTH = D_MIX - ATTN_WIDTH
N_HEADS = ATTN_WIDTH // HEAD_DIM
N_KV_HEADS = 2
GQA_GROUP = N_HEADS // N_KV_HEADS
HY_GROUP_DIM = 64
HY_GROUPS = HYENA_WIDTH // HY_GROUP_DIM
ROPE_THETA = 10000.0
ROPE_FREQS = HEAD_DIM // 4
Q_BLOCK = 128
HY_ORDER = 2
HY_SHORT = 3
HY_DIRS = 2
HY_BANDS = 16
HY_POS_DIM = 1 + 2 * HY_BANDS
HY_FILTER_HIDDEN = 64
HY_DECAY_MIN = 3.0
HY_DECAY_MAX = 15.0
N_GROUPS = 4
EXPERTS_PER_GROUP = 8
N_EXPERTS = N_GROUPS * EXPERTS_PER_GROUP
TOP_K_INNER = 2
EXPERT_FF = D_MODEL // 4
Q_DIM = N_HEADS * HEAD_DIM
KV_DIM = N_KV_HEADS * HEAD_DIM
IN_WIDTH = Q_DIM + 2 * KV_DIM + (HY_ORDER + 1) * HYENA_WIDTH
DEEPNORM_ALPHA = (2.0 * DEPTH) ** 0.25
DEEPNORM_BETA = (8.0 * DEPTH) ** -0.25
EPS = 1e-6

kernel_name = 'hybrid_gqa_hyena_hmoe_diffusion_step'

def rms_norm(x, gain):
    xf = x.astype(jnp.float32)
    y = xf * lax.rsqrt(jnp.mean(xf * xf, axis=-1, keepdims=True) + EPS)
    return (y * gain.astype(jnp.float32)).astype(x.dtype)

def layer_norm(x, gain, bias):
    xf = x.astype(jnp.float32)
    xc = xf - jnp.mean(xf, axis=-1, keepdims=True)
    var = jnp.mean(xc * xc, axis=-1, keepdims=True)
    y = xc * lax.rsqrt(var + EPS) * gain.astype(jnp.float32) + bias.astype(jnp.float32)
    return y.astype(x.dtype)

def adaln(cond, w_mod, b_mod):
    return jnp.split(jax.nn.silu(cond) @ w_mod + b_mod, 6, axis=-1)

def rope_2d(x):
    L = x.shape[1]
    n_rows = L // GRID_W
    rows = jnp.broadcast_to(jnp.arange(n_rows, dtype=jnp.float32)[:, None], (n_rows, GRID_W)).reshape(L)
    cols = jnp.broadcast_to(jnp.arange(GRID_W, dtype=jnp.float32)[None, :], (n_rows, GRID_W)).reshape(L)
    inv_freq = ROPE_THETA ** (-jnp.arange(ROPE_FREQS, dtype=jnp.float32) / ROPE_FREQS)
    ang = jnp.stack([rows[:, None] * inv_freq, cols[:, None] * inv_freq], axis=1)
    cos = jnp.cos(ang)[None, :, None]
    sin = jnp.sin(ang)[None, :, None]
    xf = x.astype(jnp.float32).reshape(x.shape[:3] + (2, 2, ROPE_FREQS))
    x1 = xf[..., 0, :]
    x2 = xf[..., 1, :]
    out = jnp.stack([x1 * cos - x2 * sin, x2 * cos + x1 * sin], axis=-2)
    return out.reshape(x.shape).astype(x.dtype)

def attend_blocked(q, k, v):
    B, Lq = q.shape[0], q.shape[1]
    nb = Lq // Q_BLOCK
    qb = q.reshape(B, nb, Q_BLOCK, N_KV_HEADS, GQA_GROUP, HEAD_DIM).transpose(1, 0, 2, 3, 4, 5)
    scale = HEAD_DIM ** -0.5

    def block(q_blk):
        s = jnp.einsum('bqkgd,bskd->bkgqs', q_blk, k, preferred_element_type=jnp.float32) * scale
        p = jax.nn.softmax(s, axis=-1).astype(v.dtype)
        return jnp.einsum('bkgqs,bskd->bqkgd', p, v)

    o = lax.map(block, qb)
    return o.transpose(1, 0, 2, 3, 4, 5).reshape(B, Lq, Q_DIM)

def hyena_filters(L, w1, b1, w2, b2, w3, freq, decay):
    f32 = jnp.float32
    t = jnp.arange(L, dtype=f32) / L
    bands = jnp.arange(1, HY_BANDS + 1, dtype=f32)
    ang = 2.0 * np.pi * t[:, None] * bands
    z = jnp.concatenate([t[:, None], jnp.sin(ang), jnp.cos(ang)], axis=-1)
    fr = freq.astype(f32)
    h = jnp.sin(fr * (z @ w1.astype(f32) + b1.astype(f32)))
    h = jnp.sin(fr * (h @ w2.astype(f32) + b2.astype(f32)))
    h = h @ w3.astype(f32)
    h = h * jnp.exp(-t[:, None] * jnp.abs(decay.astype(f32)))
    h = h.reshape(L, HY_DIRS, HY_ORDER, HYENA_WIDTH)
    g = jnp.concatenate([h[:, 0], jnp.zeros((1, HY_ORDER, HYENA_WIDTH), f32), h[:0:-1, 1]], axis=0)
    g = g * lax.rsqrt(jnp.sum(g * g, axis=0, keepdims=True) + EPS)
    return jnp.fft.rfft(g, axis=0)

def hyena_mixer(u, short_w, short_b, w1, b1, w2, b2, w3, freq, decay, skip):
    L = u.shape[1]
    up = jnp.pad(u, ((0, 0), (1, 1), (0, 0)))
    uc = up[:, :-2] * short_w[0] + up[:, 1:-1] * short_w[1] + up[:, 2:] * short_w[2] + short_b
    parts = jnp.split(uc.astype(jnp.float32), HY_ORDER + 1, axis=-1)
    spec = hyena_filters(L, w1, b1, w2, b2, w3, freq, decay)
    z = parts[0]
    for o in range(HY_ORDER):
        zc = jnp.fft.irfft(jnp.fft.rfft(z, n=2 * L, axis=1) * spec[None, :, o], n=2 * L, axis=1)[:, :L]
        z = parts[o + 1] * (zc + z * skip[o].astype(jnp.float32))
    return z.astype(u.dtype)

def hier_moe(x, grp_w, grp_b, exp_w, exp_b, w_gate, w_up, w_down):
    shp = x.shape
    xt = x.reshape(-1, D_MODEL)
    T = xt.shape[0]
    gl = (xt @ grp_w + grp_b).astype(jnp.float32)
    pg = jax.nn.softmax(gl, axis=-1)
    g_idx = jnp.argmax(gl, axis=-1)
    pg_top = jnp.take_along_axis(pg, g_idx[:, None], axis=1)[:, 0]
    el = (xt @ exp_w + exp_b).astype(jnp.float32).reshape(T, N_GROUPS, EXPERTS_PER_GROUP)
    sel = jnp.take_along_axis(el, g_idx[:, None, None], axis=1)[:, 0]
    vals, idx = lax.top_k(sel, TOP_K_INNER)
    w = pg_top[:, None] * jax.nn.softmax(vals, axis=-1)
    expert_id = g_idx[:, None] * EXPERTS_PER_GROUP + idx
    combine = jnp.sum(jax.nn.one_hot(expert_id, N_EXPERTS, dtype=jnp.float32) * w[..., None], axis=1)
    combine = combine.astype(x.dtype)
    y = jnp.zeros_like(xt)
    for e in range(N_EXPERTS):
        h = jax.nn.silu(xt @ w_gate[e]) * (xt @ w_up[e])
        y = y + combine[:, e:e + 1] * (h @ w_down[e])
    return y.reshape(shp)

def trunk_layer(x, mod, p, l, latent, ctx_k=None, ctx_v=None):
    B, L, _ = x.shape
    sh1, sc1, g1, sh2, sc2, g2 = mod
    h = x * (1 + sc1) + sh1
    proj = h @ p['w_in'][l]
    q, k, v, hy = jnp.split(proj, [Q_DIM, Q_DIM + KV_DIM, Q_DIM + 2 * KV_DIM], axis=-1)
    q = rms_norm(q.reshape(B, L, N_HEADS, HEAD_DIM), p['q_gain'][l])
    k = rms_norm(k.reshape(B, L, N_KV_HEADS, HEAD_DIM), p['k_gain'][l])
    v = v.reshape(B, L, N_KV_HEADS, HEAD_DIM)
    if latent:
        q = rope_2d(q)
        k_all = jnp.concatenate([rope_2d(k), ctx_k.astype(k.dtype)], axis=1)
        v_all = jnp.concatenate([v, ctx_v.astype(v.dtype)], axis=1)
    else:
        k_all, v_all = k, v
    attn = attend_blocked(q, k_all, v_all)
    attn = rms_norm(attn.reshape(B, L, N_HEADS, HEAD_DIM), p['attn_out_gain'][l].reshape(N_HEADS, HEAD_DIM))
    hyo = hyena_mixer(hy, p['hy_short_w'][l], p['hy_short_b'][l], p['hy_f_w1'][l], p['hy_f_b1'][l],
                      p['hy_f_w2'][l], p['hy_f_b2'][l], p['hy_f_w3'][l], p['hy_freq'][l], p['hy_decay'][l],
                      p['hy_skip'][l])
    hyo = rms_norm(hyo.reshape(B, L, HY_GROUPS, HY_GROUP_DIM), p['hy_out_gain'][l].reshape(HY_GROUPS, HY_GROUP_DIM))
    mix = jnp.concatenate([attn.reshape(B, L, ATTN_WIDTH), hyo.reshape(B, L, HYENA_WIDTH)], axis=-1) @ p['w_out'][l]
    x = layer_norm(DEEPNORM_ALPHA * x + g1 * mix, p['ln1_g'][l], p['ln1_b'][l])
    h2 = x * (1 + sc2) + sh2
    moe = hier_moe(h2, p['router_grp_w'][l], p['router_grp_b'][l], p['router_exp_w'][l], p['router_exp_b'][l],
                   p['exp_w_gate'][l], p['exp_w_up'][l], p['exp_w_down'][l])
    x = layer_norm(DEEPNORM_ALPHA * x + g2 * moe, p['ln2_g'][l], p['ln2_b'][l])
    return x, k, v

def setup_inputs(seed: int = 0) -> dict:
    key = jax.random.key(seed)
    ks = jax.random.split(key, 35)

    def nrm(i, shape, scale=1.0):
        return jax.random.normal(ks[i], shape, jnp.float32) * scale

    HY_IN = (HY_ORDER + 1) * HYENA_WIDTH
    HY_FILT_OUT = HY_DIRS * HY_ORDER * HYENA_WIDTH
    return {
        'x_prompt': nrm(0, (BATCH, SEQ, D_MODEL)),
        'x_sample': nrm(1, (DEC_BATCH, DEC_SEQ, D_MODEL)),
        'c': nrm(2, (DEC_BATCH, D_MODEL)),
        'cache_k': nrm(3, (DEC_BATCH, DEPTH, PAST_LEN, N_KV_HEADS, HEAD_DIM)),
        'cache_v': nrm(4, (DEC_BATCH, DEPTH, PAST_LEN, N_KV_HEADS, HEAD_DIM)),
        'c_ctx': nrm(5, (D_MODEL,)),
        'w_mod': nrm(6, (DEPTH, D_MODEL, 6 * D_MODEL), 0.5 * D_MODEL ** -0.5),
        'b_mod': nrm(7, (DEPTH, 6 * D_MODEL), 0.02),
        'w_in': nrm(8, (DEPTH, D_MODEL, IN_WIDTH), D_MODEL ** -0.5),
        'q_gain': 1.0 + nrm(9, (DEPTH, HEAD_DIM), 0.02),
        'k_gain': 1.0 + nrm(10, (DEPTH, HEAD_DIM), 0.02),
        'attn_out_gain': 1.0 + nrm(11, (DEPTH, ATTN_WIDTH), 0.02),
        'hy_short_w': nrm(12, (DEPTH, HY_SHORT, HY_IN), HY_SHORT ** -0.5),
        'hy_short_b': nrm(13, (DEPTH, HY_IN), 0.02),
        'hy_f_w1': nrm(14, (DEPTH, HY_POS_DIM, HY_FILTER_HIDDEN), HY_POS_DIM ** -0.5),
        'hy_f_b1': nrm(15, (DEPTH, HY_FILTER_HIDDEN), 0.1),
        'hy_f_w2': nrm(16, (DEPTH, HY_FILTER_HIDDEN, HY_FILTER_HIDDEN), HY_FILTER_HIDDEN ** -0.5),
        'hy_f_b2': nrm(17, (DEPTH, HY_FILTER_HIDDEN), 0.1),
        'hy_f_w3': nrm(18, (DEPTH, HY_FILTER_HIDDEN, HY_FILT_OUT), HY_FILTER_HIDDEN ** -0.5),
        'hy_freq': 1.0 + nrm(19, (DEPTH, HY_FILTER_HIDDEN), 0.1),
        'hy_decay': jax.random.uniform(ks[20], (DEPTH, HY_FILT_OUT), jnp.float32, HY_DECAY_MIN, HY_DECAY_MAX),
        'hy_skip': nrm(21, (DEPTH, HY_ORDER, HYENA_WIDTH), 0.5),
        'hy_out_gain': 1.0 + nrm(22, (DEPTH, HYENA_WIDTH), 0.02),
        'w_out': nrm(23, (DEPTH, D_MIX, D_MODEL), DEEPNORM_BETA * D_MIX ** -0.5),
        'ln1_g': 1.0 + nrm(24, (DEPTH, D_MODEL), 0.02),
        'ln1_b': nrm(25, (DEPTH, D_MODEL), 0.02),
        'router_grp_w': nrm(26, (DEPTH, D_MODEL, N_GROUPS), D_MODEL ** -0.5),
        'router_grp_b': nrm(27, (DEPTH, N_GROUPS), 0.01),
        'router_exp_w': nrm(28, (DEPTH, D_MODEL, N_EXPERTS), D_MODEL ** -0.5),
        'router_exp_b': nrm(29, (DEPTH, N_EXPERTS), 0.01),
        'exp_w_gate': nrm(30, (DEPTH, N_EXPERTS, D_MODEL, EXPERT_FF), D_MODEL ** -0.5),
        'exp_w_up': nrm(31, (DEPTH, N_EXPERTS, D_MODEL, EXPERT_FF), D_MODEL ** -0.5),
        'exp_w_down': nrm(32, (DEPTH, N_EXPERTS, EXPERT_FF, D_MODEL), DEEPNORM_BETA * EXPERT_FF ** -0.5),
        'ln2_g': 1.0 + nrm(33, (DEPTH, D_MODEL), 0.02),
        'ln2_b': nrm(34, (DEPTH, D_MODEL), 0.02),
    }

def reference(x_prompt, x_sample, c, cache_k, cache_v, c_ctx, w_mod, b_mod, w_in, q_gain, k_gain,
              attn_out_gain, hy_short_w, hy_short_b, hy_f_w1, hy_f_b1, hy_f_w2, hy_f_b2, hy_f_w3, hy_freq,
              hy_decay, hy_skip, hy_out_gain, w_out, ln1_g, ln1_b, router_grp_w, router_grp_b, router_exp_w,
              router_exp_b, exp_w_gate, exp_w_up, exp_w_down, ln2_g, ln2_b):
    p = {
        'w_in': w_in, 'q_gain': q_gain, 'k_gain': k_gain, 'attn_out_gain': attn_out_gain,
        'hy_short_w': hy_short_w, 'hy_short_b': hy_short_b, 'hy_f_w1': hy_f_w1, 'hy_f_b1': hy_f_b1,
        'hy_f_w2': hy_f_w2, 'hy_f_b2': hy_f_b2, 'hy_f_w3': hy_f_w3, 'hy_freq': hy_freq, 'hy_decay': hy_decay,
        'hy_skip': hy_skip, 'hy_out_gain': hy_out_gain, 'w_out': w_out, 'ln1_g': ln1_g, 'ln1_b': ln1_b,
        'router_grp_w': router_grp_w, 'router_grp_b': router_grp_b, 'router_exp_w': router_exp_w,
        'router_exp_b': router_exp_b, 'exp_w_gate': exp_w_gate, 'exp_w_up': exp_w_up,
        'exp_w_down': exp_w_down, 'ln2_g': ln2_g, 'ln2_b': ln2_b,
    }
    y_prompt = x_prompt
    ks_new = []
    vs_new = []
    for l in range(DEPTH):
        mod_ctx = adaln(c_ctx[None, None, :], w_mod[l], b_mod[l])
        y_prompt, k_l, v_l = trunk_layer(y_prompt, mod_ctx, p, l, False)
        ks_new.append(k_l)
        vs_new.append(v_l)
    new_cache_k = jnp.stack(ks_new, axis=1)
    new_cache_v = jnp.stack(vs_new, axis=1)
    y_sample = x_sample
    for l in range(DEPTH):
        mod_lat = adaln(c[:, None, :], w_mod[l], b_mod[l])
        y_sample, _, _ = trunk_layer(y_sample, mod_lat, p, l, True, cache_k[:, l], cache_v[:, l])
    return (y_prompt, y_sample, new_cache_k, new_cache_v)


_drawn_inputs = setup_inputs


def setup_inputs(seed=0):
    import zlib

    import numpy as np

    out = dict(_drawn_inputs(seed))
    spreads = {}
    factors = {'cache_k': 8.0,
     'cache_v': 8.0,
     'q_gain': 8.0,
     'attn_out_gain': 25.055,
     'hy_short_b': 4.55,
     'hy_freq': 2.88,
     'hy_out_gain': 24.241,
     'ln1_g': 2.77,
     'ln1_b': 2.704,
     'router_grp_b': 21.985,
     'router_exp_b': 25.717,
     'ln2_g': 22.378,
     'ln2_b': 22.779}
    for name, (base, spread) in spreads.items():
        noise = np.random.default_rng([zlib.crc32(name.encode()), seed]).standard_normal(out[name].shape)
        drawn = base * np.exp(spread * noise) if base else spread * noise
        out[name] = jnp.asarray(drawn.astype(out[name].dtype))
    for name, factor in factors.items():
        out[name] = (out[name] * factor).astype(out[name].dtype)
    return out
```

```python
from contextlib import ExitStack

import concourse.bass as bass
import numpy as np
from concourse import mybir

ALU = mybir.AluOpType
ACT = mybir.ActivationFunctionType
AX = mybir.AxisListType
F32 = mybir.dt.float32
F32R = mybir.dt.float32r
I32 = mybir.dt.int32

P = 128
D = 1024
KT = D // P
LAT = 1024
CTX = 128
NLAT = LAT // P
NTILE = NLAT + 1
T = LAT + CTX
HEADS, KV, HD = 8, 2, 64
GQA = HEADS // KV
QKVW = (HEADS + 2 * KV) * HD
HW = 512
IN_W = QKVW + 3 * HW
CHUNK = 384
MOD_CHUNKS = 6 * D // CHUNK
IN_CHUNKS = IN_W // CHUNK
QKV_CHUNKS = QKVW // CHUNK
FEATS = 3 * HW // P
POS = 33
HID = 64
NEXP, EPG, NGRP = 32, 8, 4
FF = 256
ROUTE_W = NGRP + NEXP
MAX_BLOCKS = 50
ALPHA = 2.0 ** 0.25
EPS = 1e-6
NCLS = 9
CCLS = 2
C1, C2, C3 = (float(np.cos(np.pi * m / 8)) for m in (1, 2, 3))
ROUND_MAGIC = 12582912.0
TWO_PI_HI = 6.28125
TWO_PI_LO = float(2 * np.pi - 6.28125)
PI_BELOW = 3.1415925
RSQRT_SEED = float(0x5F3759DF)
BIG = 1e30

N_MATS = 6 * NCLS + 4 * CCLS


def fourier_matrices():
    p = np.arange(P, dtype=np.float64)[:, None]
    q = np.arange(P, dtype=np.float64)[None, :]
    mats = []
    for k1 in range(NCLS):
        ang = 2 * np.pi * ((p * (k1 + 16 * q)) % (2 * LAT)) / (2 * LAT)
        mats += [np.cos(ang), np.sin(ang), -np.sin(ang)]
        scale = (1.0 if k1 in (0, 8) else 2.0) / (2 * LAT)
        mats += [scale * np.cos(ang).T, scale * np.sin(ang).T, -scale * np.sin(ang).T]
    for k1 in range(CCLS):
        ang = 2 * np.pi * ((p * (k1 + 2 * q)) % (2 * CTX)) / (2 * CTX)
        mats += [np.cos(ang), -np.sin(ang), np.cos(ang).T / (2 * CTX), -np.sin(ang).T / (2 * CTX)]
    return np.ascontiguousarray(np.stack(mats, 1).astype(np.float32))


def position_features():
    cols = []
    for length in (LAT, CTX):
        t = np.arange(length, dtype=np.float64) / length
        ang = 2.0 * np.pi * t[None, :] * np.arange(1, 17)[:, None]
        cols.append(np.concatenate([t[None, :], np.sin(ang), np.cos(ang)], 0))
    return np.ascontiguousarray(np.concatenate(cols, 1).astype(np.float32))


def negative_times():
    t = np.arange(P, dtype=np.float64)[:, None]
    lat = -(t + P * np.arange(NLAT)[None, :]) / LAT
    return np.ascontiguousarray(np.concatenate([lat, -t / CTX], 1).astype(np.float32))


def rotary_tables():
    t = np.arange(LAT)
    inv = 10000.0 ** (-np.arange(16) / 16.0)
    ang = np.stack([(t // 64)[:, None] * inv, (t % 64)[:, None] * inv], 1)
    cos = np.stack([np.cos(ang)] * 2, 2).reshape(LAT, HD)
    sin = np.stack([-np.sin(ang), np.sin(ang)], 2).reshape(LAT, HD)
    both = np.stack([cos, sin], 1).reshape(NLAT, P, 2, HD).transpose(1, 0, 2, 3)
    return np.ascontiguousarray(both.astype(np.float32))


def small_tables():
    eye, one = np.eye(P), np.ones((P, P))
    upper = np.triu(np.ones((P, P)), 1)
    row = np.broadcast_to(np.arange(P), (P, P))
    tok = np.arange(P)[:, None] + P * np.arange(32)[None, :]
    return np.ascontiguousarray(np.concatenate([eye, one, upper, row, tok], 1).astype(np.float32))


class Columns:

    count = 0

    def __init__(self, nc, start, end, dt=F32):
        self.nc, self.at, self.end, self.dt = nc, start, end, dt

    def take(self, width, pattern=None, rows=P, **sizes):
        assert self.at + width <= self.end, (self.at, width, self.end)
        Columns.count += 1
        with ExitStack() as place:
            if self.at:
                place.enter_context(self.nc.sbuf_tensor(f"before{Columns.count}", [P, self.at], F32))
            tensor = place.enter_context(self.nc.sbuf_tensor(f"buffer{Columns.count}", [P, width], self.dt))
        self.at += -(-width // 16) * 16
        ap = tensor[0:rows, :]
        return ap.rearrange(pattern, **sizes) if pattern else ap


def build(nc, I, O):
    ctx = ExitStack()
    with ctx:
        SB_COLS = 53000
        PS = ctx.enter_context(nc.psum_tensor("PS", [P, 8 * 512], F32))

        def bank(b, width=512, rows=P, at=0):
            return PS[0:rows, 512 * b + at:512 * b + at + width]

        def dram(name, shape, dt=F32):
            return nc.dram_tensor(name, shape, dt, kind="Internal").ap()

        mod_d = dram("mod_rows", [2, 6 * D])
        spec_d = dram("filter_spectra", [2, NCLS + CCLS, 2, P, HW])
        h2_d = dram("moe_inputs", [T, D])
        slot_y_d = dram("slot_outputs", [MAX_BLOCKS * P, D])

        sems = {}

        def sem(name):
            if name not in sems:
                sems[name] = ctx.enter_context(nc.semaphore(name))
            return sems[name]

        keep = Columns(nc, 0, 4096)
        tables = keep.take(4 * P + 32)
        ident, ones, upper, row128 = (tables[:, P * i:P * (i + 1)] for i in range(4))
        token_no = tables[:, 4 * P:4 * P + 32]
        ntime = keep.take(NTILE)
        N_COLS = 36 + 12 + 8 + 8 + 16 + 16
        cols = keep.take(N_COLS)
        taps = cols[:, 0:36].rearrange("p (f w) -> p f w", w=3)
        tap_bias = cols[:, 36:48]
        skip_col = cols[:, 48:56].rearrange("p (o c) -> p o c", o=2)
        out_gain = cols[:, 56:64]
        bmod_col = cols[:, 64:80].rearrange("p (s k) -> p s k", s=2)
        cond = cols[:, 80:96].rearrange("p (c k) -> p c k", c=2)
        cond_silu = keep.take(16, "p (k c) -> p k c", c=2)
        mod_col = keep.take(32, "p (c s k) -> p c s k", c=2, s=2)
        qk_gain = keep.take(640)
        route_bias = keep.take(ROUTE_W)
        hid_cols = keep.take(P)
        w1_sb = keep.take(HID)
        col_v = keep.take(8)
        col_t = keep.take(8)
        col_r = keep.take(16, "p (o i) -> p o i", o=2)
        col_s = keep.take(8)
        tap_s = keep.take(12 * 8, "p (f l w) -> p f l w", l=2, w=4)
        mod_ring = keep.take(2 * CHUNK, "p (r n) -> p r n", r=2)
        stat = keep.take(3 * 144, "p (a n) -> p a n", a=3)
        logits = keep.take(NTILE * ROUTE_W, "p (t e) -> p t e", t=NTILE)
        slot_token = keep.take(MAX_BLOCKS).bitcast(I32)
        control = keep.take(64, rows=1).bitcast(I32)
        slot_of = keep.take(2 * NTILE).bitcast(I32)
        mix_w = keep.take(2 * NTILE, "p (c t) -> p c t", c=2)
        bn = keep.take(16)
        token_col = keep.take(2).bitcast(I32)

        MATS0, WR0, HB0, TOP0 = 4096, 12032, 18176, 27392
        low = Columns(nc, MATS0, TOP0)
        mats = low.take(N_MATS * P, "p (m q) -> p m q", q=P)
        wring = low.take(2 * KT * CHUNK, "p (r k n) -> p r k n", r=2, k=KT)
        hbuf = low.take(2 * NTILE * HW)
        xT = hbuf.rearrange("p (k t) -> p k t", k=KT)
        hbuf = hbuf.rearrange("p (d j c) -> p d j c", d=2, j=NTILE)

        top = Columns(nc, TOP0, SB_COLS)
        h2T = top.take(T)
        w3 = top.take(4 * HW)
        decay = top.take(4 * HW)
        AF_f = top.take(16 * HW, "p (i c) -> p i c", i=16)
        TT_f = top.take(10 * HW, "p (i c) -> p i c", i=10)
        win = top.take(4 * HW, "p (r c) -> p r c", r=4)
        sq = top.take(2 * HW, "p (r c) -> p r c", r=2)
        spec_out = top.take(3 * HW, "p (r c) -> p r c", r=3)
        zeros = Columns(nc, 51000, SB_COLS).take(D)
        feats = AF_f[0:POS, 0:3, :].rearrange("p i c -> p (i c)")[:, 0:T]
        h1T = AF_f[0:HID, 3:6, :].rearrange("p i c -> p (i c)")[:, 0:T]
        arg = AF_f[0:HID, 6:9, :].rearrange("p i c -> p (i c)")[:, 0:T]
        turns = AF_f[0:HID, 9:12, :].rearrange("p i c -> p (i c)")[:, 0:T]
        norms = AF_f[:, 12:14, :]

        top = Columns(nc, TOP0, SB_COLS)
        qkv = top.take(NTILE * QKVW, "p (t n) -> p t n", t=NTILE)
        U0 = top.at
        U = [top.take(NTILE * HW, "p (t n) -> p t n", t=NTILE) for _ in range(3)]
        TAIL0 = top.at
        uc = top.take(2 * T, "p (r t) -> p r t", r=2)

        low = Columns(nc, WR0, TOP0)
        AF_h = low.take(16 * HW, "p (i c) -> p i c", i=16)
        TT_h = low.take(10 * HW, "p (i c) -> p i c", i=10)
        prod = low.take(4 * HW, "p (i c) -> p i c", i=4)
        tail = Columns(nc, TAIL0, SB_COLS)
        gbuf = tail.take(4 * HW, "p (r i c) -> p r i c", r=2, i=2)
        wbuf = tail.take(4 * HW, "p (r i c) -> p r i c", r=2, i=2)

        low = Columns(nc, MATS0, TOP0, F32R)
        qT = low.take(HEADS * T, "p (h t) -> p h t", h=HEADS)
        kT = low.take(4 * 10 * P, "p (s v t) -> p s v t", s=2, v=KV)
        q_split = low.take(2 * 2 * HEADS * HD, "p (r h s d) -> p r h s d", r=2, h=HEADS, s=2)
        k_split = low.take(2 * 2 * KV * 2 * HD, "p (r s v c d) -> p r s v c d", r=2, s=2, v=KV, c=2)
        low = Columns(nc, low.at, TOP0)
        probs = low.take(2 * NTILE * P, "p (r n) -> p r n", r=2)
        probsT = low.take(2 * NTILE * P, "p (r t n) -> p r t n", r=2, t=NTILE)
        qk_work = low.take(640)
        tail = Columns(nc, TAIL0, SB_COLS)
        attn = tail.take(NTILE * HW, "p (t n) -> p t n", t=NTILE)
        gates = Columns(nc, U0 + NTILE * HW, TAIL0)
        cache_k = gates.take(P)
        cache_v = gates.take(P)
        rot = gates.take(NLAT * 2 * HD, "p (t s d) -> p t s d", t=NLAT, s=2)
        nmax = gates.take(72)
        psums = gates.take(72)
        precip = gates.take(72)
        rstd_qk = gates.take(90)
        ss_qk = gates.take(90)
        ss_tmp = gates.take(90)

        low = Columns(nc, MATS0, U0)
        rows = low.take(12 * D, "p (r n) -> p r n", r=12)
        ROW_OF = {"sh2": 0, "sc2": 1, "g1": 2, "g2": 3}
        ln_rows = rows[:, 8:12, :]
        w_out = low.take(KT * D, "p (k n) -> p k n", k=KT)
        mixT = low.take(2 * KT * P, "p (r k n) -> p r k n", r=2, k=KT)
        xres = low.take(2 * D, "p (r n) -> p r n", r=2)
        resid = low.take(D)
        xnorm = low.take(D)
        h2buf = low.take(2 * D, "p (r n) -> p r n", r=2)
        h2Tt = low.take(KT * P, "p (k n) -> p k n", k=KT)
        route_w = low.take(KT * ROUTE_W, "p (k n) -> p k n", k=KT)
        x1 = Columns(nc, U0 + NTILE * HW, TAIL0).take(NTILE * D, "p (t n) -> p t n", t=NTILE)

        rt = Columns(nc, MATS0 + 12 * D, U0)
        r_eq = rt.take(NTILE * NGRP, "p (t g) -> p t g", t=NTILE)
        r_g = rt.take(NTILE * NGRP, "p (t g) -> p t g", t=NTILE)
        r_exp = rt.take(NTILE * NGRP, "p (t g) -> p t g", t=NTILE)
        r_max = rt.take(NTILE)
        r_min = rt.take(NTILE)
        r_pg = rt.take(NTILE)
        r_v = rt.take(2 * NTILE, "p (c t) -> p c t", c=2)
        r_d = rt.take(NTILE)
        r_prod = rt.take(NTILE * NEXP, "p (t g e) -> p t g e", t=NTILE, g=NGRP)
        r_sel = rt.take(NTILE * EPG, "p (t e) -> p t e", t=NTILE)
        r_cand = rt.take(NTILE * EPG, "p (t e) -> p t e", t=NTILE)
        r_pick = rt.take(2 * NTILE * EPG, "p (c t e) -> p c t e", c=2, t=NTILE)
        r_mask = rt.take(2 * NTILE * NEXP, "p (c t n) -> p c t n", c=2, t=NTILE)
        r_all = rt.take(NTILE * NEXP, "p (t n) -> p t n", t=NTILE)
        r_before = rt.take((NTILE + 1) * NEXP, "p (t n) -> p t n", t=NTILE + 1)
        r_count = rt.take(NEXP)
        r_blocks = rt.take(NEXP)
        r_scan = rt.take(2 * NEXP, "p (r n) -> p r n", r=2)
        r_base = rt.take(NEXP)
        r_slot = rt.take(NTILE * NEXP, "p (t n) -> p t n", t=NTILE)
        r_pos = rt.take(2 * NTILE)
        r_int = rt.take(4 * NTILE).bitcast(I32)
        r_rowblk = rt.take(4 * NTILE, "p (a n) -> p a n", a=2)
        r_hot = rt.take(2 * P, "p (r n) -> p r n", r=2)
        r_tok = rt.take(2 * MAX_BLOCKS, "p (r n) -> p r n", r=2)
        r_cmp = rt.take(MAX_BLOCKS * NEXP, "p (b n) -> p b n", b=MAX_BLOCKS)
        r_eid = rt.take(64)

        ex = Columns(nc, MATS0 + 12 * D, U0 + NTILE * HW)
        w_gu = ex.take(2 * 2 * KT * FF, "p (r g k f) -> p r g k f", r=2, g=2, k=KT)
        w_dn = ex.take(2 * 2 * D, "p (r s n) -> p r s n", r=2, s=2)
        ybuf = ex.take(2 * D, "p (r n) -> p r n", r=2)
        hT = ex.take(2 * 2 * P, "p (r s n) -> p r s n", r=2, s=2)
        gate_act = ex.take(2 * 2 * P, "p (r s n) -> p r s n", r=2, s=2)
        ex = Columns(nc, TAIL0, SB_COLS)
        xg = ex.take(2 * D, "p (r n) -> p r n", r=2)
        xgT = ex.take(2 * KT * P, "p (r k n) -> p r k n", r=2, k=KT)

        fin = Columns(nc, MATS0 + 12 * D, U0)
        yg = fin.take(4 * D, "p (r c n) -> p r c n", r=2, c=2)
        acc = fin.take(2 * D, "p (r n) -> p r n", r=2)
        ynorm = fin.take(2 * D, "p (r n) -> p r n", r=2)

        rs = {"spec": [sem(f"spectrum_stored{r}") for r in range(3)]}

        def filter_items(o):
            return [(18 * o + 2 * j + d, j, d) for j in range(NTILE) for d in range(2)]

        CLS_ORDER = (0, 8, 4, 2, 6, 1, 3, 5, 7)
        PART_OF = {0: 1, 8: 1, 4: 1, 2: 2, 6: 2}

        def spectrum_items(o):
            out = []
            for part in range(2):
                for cls in [*range(NCLS, NCLS + CCLS), *CLS_ORDER]:
                    out.append((22 * o + len(out), part, cls))
            return out

        N_SPEC = 2 * 22
        SPEC_STORED = [16 * len(range(r, N_SPEC, 3)) for r in range(3)]

        def mat(cls, kind):
            if cls < NCLS:
                return mats[:, 6 * cls + kind, :]
            return mats[:, 6 * NCLS + 4 * (cls - NCLS) + {0: 0, 2: 1, 3: 2, 5: 3}[kind], :]

        ATT = [(h, t) for h in range(HEADS) for t in range(NLAT)] + [(h, NLAT) for h in range(HEADS)]
        block = ctx.enter_context(nc.Block())

        @block.sync
        def _(sp):
            def load(dst, src, s, **kw):
                return sp.dma_start(dst, src, **kw).then_inc(sem(s), 16)

            load(cols, I["cols"], "small_loaded")
            load(tables, I["tables"], "small_loaded")
            load(ntime, I["ntime"], "small_loaded")
            load(feats, I["feats"], "small_loaded")
            load(w1_sb[0:POS, :], I["hy_f_w1"], "small_loaded")
            load(hid_cols[0:HID, 0:HID + 3], I["hid"], "small_loaded")
            load(w3[0:HID, :], I["hy_f_w3"], "small_loaded")
            load(decay, I["hy_decay"].partition_broadcast(P), "small_loaded")
            load(mats[:, 0:N_MATS // 2, :], I["mats"][:, 0:N_MATS // 2, :], "mats_loaded")
            load(mats[:, N_MATS // 2:, :], I["mats"][:, N_MATS // 2:, :], "mats_loaded")
            load(qk_gain, I["qk_gain"].partition_broadcast(P), "gains_loaded")
            load(route_bias, I["route_bias"].partition_broadcast(P), "gains_loaded")
            w_mod = I["w_mod"].rearrange("(p k) n -> p k n", k=KT)
            for c in range(MOD_CHUNKS):
                if c >= 2:
                    sp.wait_ge(sem("mod_product"), c - 1)
                load(wring[:, c % 2, :, :], w_mod[:, :, CHUNK * c:CHUNK * (c + 1)], f"w_loaded{c % 2}")
            w_in = I["w_in"].rearrange("(p k) n -> p k n", k=KT)

            def load_w_in(c):
                load(wring[:, c % 2, :, :], w_in[:, :, CHUNK * c:CHUNK * (c + 1)], f"w_loaded{c % 2}")

            for c in range(2):
                sp.wait_ge(sem("mod_product"), MOD_CHUNKS - 1 + c)
                load_w_in(c)
            for r in range(2):
                sp.wait_ge(sem(f"mod_stored{r}"), 16 * (MOD_CHUNKS // 2))
            for c in range(2):
                for s in range(2):
                    load(mod_col[:, c, s, :], mod_d[c, D * s:D * (s + 1)].rearrange("(p k) -> p k", k=KT),
                         "mod_col_loaded")
            sp.wait_ge(sem("tiles_transformed"), 12)
            sp.wait_ge(sem("spectrum_product"), 22 + 13)
            load(xT[:, :, :], I["xT"].rearrange("(p k) t -> p k t", k=KT), "x_loaded")
            for c in range(2, IN_CHUNKS):
                if c < 4:
                    sp.wait_ge(sem("qkv_product"), NTILE * (c - 1))
                else:
                    sp.wait_ge(sem("feature_product"), 3 * (c - 3))
                load_w_in(c)
            sp.wait_ge(sem("zeros_ready"), 1)
            for b in range(0, MAX_BLOCKS, 10):
                load(slot_y_d[P * b:P * (b + 10), :].rearrange("(b p) n -> p b n", p=P),
                     zeros.unsqueeze(1).broadcast_to([P, 10, D]), "slots_zeroed")
            for r in range(3):
                sp.wait_ge(rs["spec"][r], SPEC_STORED[r])
            sp.wait_ge(sem("tokens_product"), 3 * FEATS)
            for q in range(2 * (NCLS + CCLS)):
                if q >= 2:
                    sp.wait_ge(sem("w_ready"), q - 1)
                o, idx = divmod(q, NCLS + CCLS)
                cls = CLS_ORDER[idx] if idx < NCLS else idx
                load(gbuf[:, q % 2, :, :], spec_d[o, cls].rearrange("i p c -> p i c"), f"g_loaded{q % 2}")
            sp.wait_ge(sem("hyena_done"), 1)
            load(cache_k, I["cache_k"], "cache_loaded")
            load(cache_v, I["cache_v"], "cache_loaded")
            load(rot, I["rot"], "cache_loaded")
            sp.wait_ge(sem("split_ready"), 10)
            load(O["new_k"], qkv[:, NLAT, HEADS * HD:(HEADS + KV) * HD], "out_stored")
            load(O["new_v"], qkv[:, NLAT, (HEADS + KV) * HD:QKVW], "out_stored")
            sp.wait_ge(sem("out_stored"), 32)
            sp.wait_ge(sem("attn_out"), len(ATT))
            for c in range(2):
                for i, s in enumerate((3, 4, 2, 5)):
                    load(rows[:, 4 * c + i, :], mod_d[c, D * s:D * (s + 1)].partition_broadcast(P), "rows_loaded")
            load(ln_rows[:, 0, :], I["ln1_g"].partition_broadcast(P), "rows_loaded")
            load(ln_rows[:, 1, :], I["ln1_b"].partition_broadcast(P), "rows_loaded")
            load(w_out[:, 0, :], I["b_mod"][D * 3:D * 4].partition_broadcast(P), "bias_loaded")
            load(w_out[:, 1, :], I["b_mod"][D * 4:D * 5].partition_broadcast(P), "bias_loaded")
            load(w_out[:, 2, :], I["b_mod"][D * 2:D * 3].partition_broadcast(P), "bias_loaded")
            load(w_out[:, 3, :], I["b_mod"][D * 5:D * 6].partition_broadcast(P), "bias_loaded")
            load(route_w, I["route_w"].rearrange("(k p) n -> p k n", p=P), "route_w_loaded")
            load(ln_rows[:, 2, :], I["ln2_g"].partition_broadcast(P), "ln2_loaded")
            load(ln_rows[:, 3, :], I["ln2_b"].partition_broadcast(P), "ln2_loaded")
            x_tok = I["x_tok"].rearrange("(t p) n -> t p n", p=P)
            for t in range(2):
                load(xres[:, t, :], x_tok[t], f"xres_loaded{t % 2}")
            sp.wait_ge(sem("rows_ready"), 1)
            load(w_out[:, :, :], I["w_out"].rearrange("(k p) n -> p k n", p=P), "w_out_loaded")
            for t in range(NTILE):
                if t >= 2:
                    sp.wait_ge(sem("resid_ready"), t - 1)
                    load(xres[:, t % 2, :], x_tok[t], f"xres_loaded{t % 2}")
                sp.wait_ge(sem("h2_ready"), t + 1)
                load(h2_d[P * t:P * (t + 1), :], h2buf[:, t % 2, :], f"h2_stored{t % 2}")
            sp.wait_ge(sem("route_done"), 1)
            pairs = sp.value_load(control[0:1, 60:61], min_val=1, max_val=MAX_BLOCKS // 2)
            with sp.Fori(0, pairs) as i:
                for u in range(2):
                    e = sp.value_load(control[0:1, bass.ds(2 * i + u, 1)], min_val=0, max_val=NEXP - 1)
                    sp.wait_ge(sem("gate_up_product"), 2 * i + u + 1)
                    for g, name in enumerate(("exp_w_gate", "exp_w_up")):
                        load(w_gu[:, u, g, :, :].rearrange("p k f -> p (k f)"),
                             I[name][bass.ds(e, 1), :, :].rearrange("e (p k) f -> p (e k f)", k=KT), f"we_loaded{u}")
                for u in range(2):
                    e = sp.value_load(control[0:1, bass.ds(2 * i + u, 1)], min_val=0, max_val=NEXP - 1)
                    sp.wait_ge(sem("block_done"), 2 * i + u + 1)
                    load(w_dn[:, u, :, :].rearrange("p s n -> p (s n)"),
                         I["exp_w_down"][bass.ds(e, 1), :, :].rearrange("e (p s) n -> p (e s n)", s=2), f"wd_loaded{u}")
            for t in range(NTILE):
                sp.wait_ge(sem("y_ready"), t + 1)
                out = O["lat"][P * t:P * (t + 1), :] if t < NLAT else O["ctx"]
                load(out, ynorm[:, t % 2, :], f"y_stored{t % 2}")
            sp.wait_ge(sem("y_stored0"), 16 * 5)
            sp.wait_ge(sem("y_stored1"), 16 * 4)

        @block.gpsimd
        def _(pool):
            pool.memset(h2T[HID:P, :], 0.0).then_inc(sem("pads_zero"), 1)
            pool.memset(w3[HID:P, :], 0.0).then_inc(sem("pads_zero"), 1)
            pool.wait_ge(sem("pads_zero"), 2)
            pool.memset(zeros, 0.0).then_inc(sem("zeros_ready"), 1)
            pool.wait_ge(sem("rows_loaded"), 16 * 10)
            pool.wait_ge(sem("bias_loaded"), 16 * 4)
            for i in range(4):
                for c in range(2):
                    pool.tensor_tensor(rows[:, 4 * c + i, :], rows[:, 4 * c + i, :], w_out[:, i, :],
                                       ALU.add).then_inc(sem("rows_biased"), 1)
            pool.wait_ge(sem("rows_biased"), 8)
            for c in range(2):
                last = pool.tensor_scalar(rows[:, 4 * c + 1, :], rows[:, 4 * c + 1, :], 1.0, None, ALU.add)
                last.then_inc(sem("rows_biased"), 1)
            pool.wait_ge(sem("rows_biased"), 10)
            pool.sem_inc(sem("rows_ready"), 1)
            n = 0
            for t in range(NTILE):
                c = 4 * (t == NLAT)
                pool.wait_ge(sem("xnorm_ready"), t + 1)
                pool.tensor_tensor(x1[:, t, :], xnorm, ln_rows[:, 0, :], ALU.mult).then_inc(sem("pool_step"), 1)
                pool.wait_ge(sem("pool_step"), n + 1)
                pool.tensor_tensor(x1[:, t, :], x1[:, t, :], ln_rows[:, 1, :], ALU.add).then_inc(sem("pool_step"), 1)
                pool.wait_ge(sem("pool_step"), n + 2)
                if t >= 2:
                    pool.wait_ge(sem(f"h2_stored{t % 2}"), 16 * (t // 2))
                    pool.wait_ge(sem("h2T_product"), t - 1)
                pool.tensor_tensor(h2buf[:, t % 2, :], x1[:, t, :], rows[:, c + 1, :], ALU.mult).then_inc(sem("pool_step"), 1)
                pool.wait_ge(sem("pool_step"), n + 3)
                pool.tensor_tensor(h2buf[:, t % 2, :], h2buf[:, t % 2, :], rows[:, c, :], ALU.add).then_inc(sem("h2_ready"), 1)
                n += 3
            pool.wait_ge(sem("ln2_loaded"), 32)
            pool.wait_ge(sem("h2_stored0"), 16 * 5)
            pool.wait_ge(sem("h2_stored1"), 16 * 4)
            pool.wait_ge(sem("route_done"), 1)
            pairs = pool.value_load(control[0:1, 60:61], min_val=1, max_val=MAX_BLOCKS // 2)
            with pool.Fori(0, pairs) as i:
                for u in range(2):
                    pool.wait_ge(sem("x_transposed"), 2 * i + u + 1)
                    pool.tensor_copy(token_col[:, u:u + 1], slot_token[:, bass.ds(2 * i + u, 1)]).then_inc(sem("token_col_ready"), 1)
                    pool.wait_ge(sem("token_col_ready"), 2 * i + u + 1)
                    pool.sem_inc(sem("gather_started"), 1)
                    pool.indirect_dma_start(
                        out=xg[:, u, :], out_offset=None, in_=h2_d[:, :],
                        in_offset=bass.IndirectOffsetOnAxis(ap=token_col[:, u:u + 1], axis=0)).then_inc(sem(f"xg_loaded{u}"), 16)
            for u in range(2):
                pool.wait_ge(sem(f"slot_y_stored{u}"), 16 * pairs + 16)
            pool.sem_inc(sem("gather_started"), 1)
            for t in range(NTILE + 1):
                if t < NTILE:
                    if t >= 2:
                        pool.wait_ge(sem("acc_ready"), t - 1)
                    for c in range(2):
                        at = NTILE * c + t
                        pool.indirect_dma_start(
                            out=yg[:, t % 2, c, :], out_offset=None, in_=slot_y_d[:, :],
                            in_offset=bass.IndirectOffsetOnAxis(ap=slot_of[:, at:at + 1], axis=0),
                        ).then_inc(sem(f"yg_loaded{t % 2}"), 16)
                if t:
                    y = ynorm[:, (t - 1) % 2, :]
                    pool.wait_ge(sem("ynorm_ready"), t)
                    pool.tensor_tensor(y, y, ln_rows[:, 2, :], ALU.mult).then_inc(sem("pool_step"), 1)
                    n += 1
                    pool.wait_ge(sem("pool_step"), n)
                    pool.tensor_tensor(y, y, ln_rows[:, 3, :], ALU.add).then_inc(sem("y_ready"), 1)

        @block.scalar
        def _(act):
            steps = [0]

            def own(ins):
                steps[0] += 1
                ins.then_inc(sem("act_step"), 1)
                act.wait_ge(sem("act_step"), steps[0])

            act.wait_ge(sem("small_loaded"), 16 * 8)
            act.activation(cond_silu[:, :, :], cond.rearrange("p c k -> p k c"), ACT.Silu).then_inc(sem("cond_ready"), 1)
            own(act.activation(decay, decay, ACT.Abs))
            for layer in range(2):
                act.wait_ge(sem("arg_ready"), layer + 1)
                dst = h1T if layer == 0 else h2T[0:HID, :]
                act.activation(dst, arg, ACT.Sin).then_inc(sem("sine_ready"), 1)

            def window(n, j, d, o):
                if n >= 4:
                    act.wait_ge(sem("taps_ready"), n - 3)
                act.activation(win[:, n % 4, :], decay[:, 2 * HW * d + HW * o:2 * HW * d + HW * (o + 1)], ACT.Exp,
                               scale=ntime[:, j:j + 1]).then_inc(sem("window_ready"), 1)

            for o in range(2):
                items = filter_items(o)
                for n, j, d in items[:2]:
                    window(n, j, d, o)
                for i, (n, j, d) in enumerate(items):
                    if i + 2 < len(items):
                        window(*items[i + 2], o)
                    act.wait_ge(sem("taps_ready"), n + 1)
                    if n >= 2:
                        act.wait_ge(sem("norm_product"), n - 1)
                    act.activation(sq[:, n % 2, :], hbuf[:, d, j, :], ACT.Square).then_inc(sem("square_ready"), 1)
                for c in range(8 * o, 8 * o + 8):
                    act.wait_ge(sem("mod_product"), c + 1)
                    if c >= 2:
                        act.wait_ge(sem(f"mod_stored{c % 2}"), 16 * (c // 2))
                    act.copy(mod_ring[0:2, c % 2, :], bank(3 + c % 2, CHUNK, rows=2)).then_inc(sem("mod_copied"), 1)
                    act.wait_ge(sem("mod_copied"), c + 1)
                    act.dma_start(mod_d[:, CHUNK * c:CHUNK * (c + 1)], mod_ring[0:2, c % 2, :]).then_inc(sem(f"mod_stored{c % 2}"), 16)
                for m, part, cls in spectrum_items(o):
                    act.wait_ge(sem("spectrum_product"), m + 1)
                    if m >= 3:
                        act.wait_ge(rs["spec"][m % 3], 16 * (m // 3))
                    act.copy(spec_out[:, m % 3, :], bank(m % 3)).then_inc(sem("spectrum_copied"), 1)
                    act.wait_ge(sem("spectrum_copied"), m + 1)
                    act.dma_start(spec_d[o, cls, part], spec_out[:, m % 3, :]).then_inc(rs["spec"][m % 3], 16)

            for m in range(QKV_CHUNKS * NTILE):
                c, t = divmod(m, NTILE)
                act.wait_ge(sem("qkv_product"), m + 1)
                act.copy(qkv[:, t, CHUNK * c:CHUNK * (c + 1)], bank(m % 4, CHUNK)).then_inc(sem("qkv_copied"), 1)
            for f in range(FEATS):
                for i, tiles in enumerate(((0, 4), (4, 8), (8, 9))):
                    g = 3 * f + i
                    n = tiles[1] - tiles[0]
                    act.wait_ge(sem("tokens_product"), g + 1)
                    act.copy(U[f // 4][:, tiles[0]:tiles[1], P * (f % 4):P * (f % 4 + 1)],
                             bank(6 + g % 2, P * n).rearrange("p (t c) -> p t c", t=n)).then_inc(sem("tokens_copied"), 1)

            for o in range(2):
                for idx, k in enumerate(CLS_ORDER):
                    act.wait_ge(sem("inverse_product"), 11 * o + idx + 1)
                    b = 4 + 2 * ((NCLS * o + idx) % 2)
                    if k in (0, 8):
                        ins = act.copy(AF_h[:, k, :], bank(b))
                    else:
                        ins = act.copy(AF_h[:, k:k + 9:8, :], PS[:, 512 * b:512 * (b + 2)].rearrange("p (i c) -> p i c", i=2))
                    ins.then_inc(sem("inverse_copied"), 1)

            act.wait_ge(sem("hyena_done"), 1)
            for t in range(NTILE):
                if t >= 2:
                    act.wait_ge(sem("qk_summed"), t - 1)
                act.activation(probs[:, t % 2, 0:640], qkv[:, t, 0:640], ACT.Square).then_inc(sem("qk_squared"), 1)
            for s in range(10):
                b = 3 * (s % 2)
                act.wait_ge(sem("qk_transposed"), s + 1)
                tile = s if s < 8 else NLAT
                if s != 8:
                    act.copy(qT[:, :, P * tile:P * (tile + 1)],
                             PS[:, 512 * b:512 * (b + 2)].rearrange("p (h t) -> p h t", h=HEADS))
                act.copy(kT[:, :, :, P * s:P * (s + 1)],
                         bank(b + 2).rearrange("p (s v t) -> p s v t", s=2, v=KV)).then_inc(sem("qk_copied"), 1)

            def exponent(i):
                h, t = ATT[i]
                n = NTILE * P if t < NLAT else P
                act.wait_ge(sem("max_ready"), i + 1)
                if i >= 2:
                    act.wait_ge(sem("probs_transposed"), i - 1)
                act.activation(probs[:, i % 2, 0:n], PS[:, 0:n], ACT.Exp, bias=nmax[:, i:i + 1], scale=1.0,
                               accum_out=psums[:, i:i + 1]).then_inc(sem("exp_ready"), 1)

            exponent(0)
            for i in range(len(ATT)):
                if i + 1 < len(ATT):
                    exponent(i + 1)
                h, t = ATT[i]
                n = 4 if t < NLAT else 1
                act.wait_ge(sem("probs_transposed"), i + 1)
                if i >= 2:
                    act.wait_ge(sem("attn_product"), i - 1)
                act.copy(probsT[:, i % 2, 0:n, :], bank(3, P * n).rearrange("p (t n) -> p t n", t=n)).then_inc(sem("probsT_a"), 1)

            act.wait_ge(sem("attn_out"), len(ATT))
            for n in range(2 * NTILE):
                t, src = divmod(n, 2)
                if n >= 2:
                    act.wait_ge(sem("mix_summed"), n - 1)
                act.activation(h2buf[:, n % 2, 0:HW], (attn, U[0])[src][:, t, :], ACT.Square).then_inc(sem("mix_squared"), 1)

            def gain_half(t):
                act.wait_ge(sem("mix_transposed"), t + 1)
                if t >= 2:
                    act.wait_ge(sem("mix_product"), t - 1)
                for k in range(4):
                    ins = act.activation(mixT[:, t % 2, k, :], bank(0, P, at=P * k), ACT.Copy, scale=out_gain[:, k:k + 1])
                ins.then_inc(sem("mixT_a"), 1)

            gain_half(0)
            for step in range(NTILE + 2):
                if step + 1 < NTILE:
                    gain_half(step + 1)
                if step < 2:
                    continue
                t = step - 2
                act.wait_ge(sem("h2T_product"), t + 1)
                if t >= 1:
                    act.wait_ge(sem("logit_product"), t)
                act.copy(h2Tt[:, :, :], PS[:, 1024:2048].rearrange("p (k n) -> p k n", k=KT)).then_inc(sem("h2T_ready"), 1)
            act.wait_ge(sem("group_shifted"), 1)
            act.activation(r_exp[:, :, :], r_g[:, :, :], ACT.Exp).then_inc(sem("group_exp"), 1)
            act.wait_ge(sem("pair_shifted"), 1)
            act.activation(r_d, r_d, ACT.Exp).then_inc(sem("pair_exp"), 1)

            act.wait_ge(sem("route_done"), 1)
            pairs = act.value_load(control[0:1, 60:61], min_val=1, max_val=MAX_BLOCKS // 2)
            for u in range(2):
                act.sem_inc(sem(f"slot_y_stored{u}"), 16)
            act.sem_inc(sem("y_a"), 2)
            with act.Fori(0, pairs) as i:
                for u in range(2):
                    act.wait_ge(sem("gate_up_product"), 2 * i + u + 3)
                    act.activation(gate_act[:, u, :, :], bank(4 + u, 256).rearrange("p (s n) -> p s n", s=2),
                                   ACT.Silu).then_inc(sem("gate_ready"), 1)
                for u in range(2):
                    act.wait_ge(sem("block_done"), 2 * i + u + 3)
                    act.wait_ge(sem(f"slot_y_stored{u}"), 16 * i + 16)
                    act.copy(ybuf[:, u, 0:512], bank((6, 2)[u])).then_inc(sem("y_a"), 1)
                    act.wait_ge(sem("y_a"), 2 * i + u + 3)
                    act.wait_ge(sem("y_d"), 2 * i + u + 3)
                    act.dma_start(slot_y_d[bass.ds(256 * i + P * u, P), :], ybuf[:, u, :]).then_inc(sem(f"slot_y_stored{u}"), 16)

        @block.tensor
        def _(pe):
            def mm(out, lhsT, rhs, start=True, stop=True):
                return nc.tensor.matmul(out, lhsT, rhs, start=start, stop=stop)

            def turn(out, in_):
                return nc.tensor.transpose(out, in_, ident)

            pe.wait_ge(sem("small_loaded"), 16 * 8)
            for layer in range(2):
                w = w1_sb[0:POS, :] if layer == 0 else hid_cols[0:HID, 0:HID]
                x = feats if layer == 0 else h1T
                if layer:
                    pe.wait_ge(sem("sine_ready"), 1)
                for c in range(3):
                    n = min(512, T - 512 * c)
                    last = mm(bank(c, n, rows=HID), w, x[:, 512 * c:512 * c + n])
                last.then_inc(sem("hidden_product"), 1)
            pe.wait_ge(sem("sine_ready"), 2)
            pe.wait_ge(sem("pads_zero"), 2)
            pe.wait_ge(sem("mats_loaded"), 32)

            def norm(n, j):
                pe.wait_ge(sem("square_ready"), n + 1)
                b, first, last = (5, n % 18 == 0, n % 18 == 15) if j < NLAT else (6, n % 18 == 16, n % 18 == 17)
                mm(bank(b), ones, sq[:, n % 2, :], first, last).then_inc(sem("norm_product"), 1)

            def modulation(c):
                pe.wait_ge(sem(f"w_loaded{c % 2}"), 16 * (c // 2 + 1))
                if c >= 2:
                    pe.wait_ge(sem("mod_copied"), c - 1)
                for k in range(KT):
                    last = mm(bank(3 + c % 2, CHUNK, rows=2), cond_silu[:, k, :], wring[:, c % 2, k, :], k == 0, k == KT - 1)
                last.then_inc(sem("mod_product"), 1)

            for o in range(2):
                items = filter_items(o)
                if o:
                    pe.wait_ge(sem("mod_copied"), 8)
                    pe.wait_ge(sem("skip_added"), 1)
                for i, (n, j, d) in enumerate(items):
                    if n >= 2:
                        pe.wait_ge(sem("taps_ready"), n - 1)
                    mm(bank(3 + n % 2), h2T[:, P * j:P * (j + 1)],
                       w3[:, 2 * HW * d + HW * o:2 * HW * d + HW * (o + 1)]).then_inc(sem("taps_product"), 1)
                    if i >= 2:
                        norm(*items[i - 2][:2])
                norm(*items[16][:2])
                norm(*items[17][:2])
                pe.wait_ge(sem("norms_ready"), o + 1)
                for i in range(8):
                    last = mm(bank(7, 1, at=i), norms[:, i // 4, P * (i % 4):P * (i % 4 + 1)], ident[:, 0:1])
                last.then_inc(sem("norm_col"), 1)
                pe.wait_ge(sem("taps_ready"), 18 * (o + 1))
                pe.wait_ge(sem("cond_ready"), 1)
                for c in range(8 * o, 8 * o + 4):
                    modulation(c)
                pe.wait_ge(sem("skip_scaled"), o + 1)
                for i in range(8):
                    last = mm(bank(7 if i < 4 else 6, P, rows=1, at=P * (i % 4)), col_s[:, i:i + 1], ident)
                last.then_inc(sem("skip_row"), 1)
                for c in range(8 * o + 4, 8 * o + 8):
                    modulation(c)
                for m, part, cls in spectrum_items(o):
                    pe.wait_ge(sem("tiles_transformed"), 3 * (2 * o + part) + (PART_OF.get(cls, 3) if cls < NCLS else 1))
                    if m >= 3:
                        pe.wait_ge(sem("spectrum_copied"), m - 2)
                    out = bank(m % 3)
                    if cls >= NCLS:
                        last = mm(out, mat(cls, 2 * part), hbuf[:, part, NLAT, :])
                    elif cls in (0, 8):
                        last = mm(out, mat(cls, 2 * part), AF_f[:, cls, :])
                    elif part == 0:
                        mm(out, mat(cls, 0), AF_f[:, cls, :], True, False)
                        last = mm(out, mat(cls, 1), AF_f[:, 8 + cls, :], False, True)
                    else:
                        mm(out, mat(cls, 2), AF_f[:, cls, :], True, False)
                        last = mm(out, mat(cls, 0), AF_f[:, 8 + cls, :], False, True)
                    last.then_inc(sem("spectrum_product"), 1)

            pe.wait_ge(sem("spectrum_copied"), N_SPEC)
            pe.wait_ge(sem("mod_copied"), MOD_CHUNKS)
            pe.wait_ge(sem("hT_ready"), 1)
            for m in range(QKV_CHUNKS * NTILE):
                c, t = divmod(m, NTILE)
                pe.wait_ge(sem(f"w_loaded{c % 2}"), 16 * (9 + c // 2))
                if m >= 4:
                    pe.wait_ge(sem("qkv_copied"), m - 3)
                for k in range(KT):
                    last = mm(bank(m % 4, CHUNK), xT[:, k, P * t:P * (t + 1)], wring[:, c % 2, k, :], k == 0, k == KT - 1)
                last.then_inc(sem("qkv_product"), 1)
            pe.wait_ge(sem("qkv_copied"), QKV_CHUNKS * NTILE)

            def to_tokens(f):
                pe.wait_ge(sem("conv_ready"), f + 1)
                for i, tiles in enumerate((range(0, 4), range(4, 8), range(8, 9))):
                    g = 3 * f + i
                    if g >= 2:
                        pe.wait_ge(sem("tokens_copied"), g - 1)
                    for a, t in enumerate(tiles):
                        last = turn(bank(6 + g % 2, P, at=P * a), uc[:, f % 2, P * t:P * (t + 1)])
                    last.then_inc(sem("tokens_product"), 1)

            for f in range(FEATS):
                c = QKV_CHUNKS + f // 3
                b = 3 * (f % 2)
                pe.wait_ge(sem(f"w_loaded{c % 2}"), 16 * (9 + c // 2))
                if f >= 2:
                    pe.wait_ge(sem("conv_ready"), f - 1)
                for part, (t0, t1) in enumerate(((0, 512), (512, 1024), (1024, T))):
                    for k in range(KT):
                        last = mm(bank(b + part, t1 - t0), wring[:, c % 2, k, P * (f % 3):P * (f % 3 + 1)], xT[:, k, t0:t1],
                                  k == 0, k == KT - 1)
                last.then_inc(sem("feature_product"), 1)
                if f:
                    to_tokens(f - 1)
            to_tokens(FEATS - 1)

            def forward(o, idx):
                q = 11 * o + idx
                b = 2 * (q % 2)
                k = CLS_ORDER[idx] if idx < NCLS else idx
                pe.wait_ge(sem("z_transformed"), 3 * o + (PART_OF.get(k, 3) if k < NCLS else 1))
                if q >= 2:
                    pe.wait_ge(sem("w_ready"), q - 1)
                if k in (0, 8) or k >= NCLS:
                    z = AF_h[:, k, :] if k < NCLS else U[0][:, NLAT, :]
                    mm(bank(b), mat(k, 0), z)
                    last = mm(bank(b + 1), mat(k, 2), z)
                else:
                    mm(bank(b), mat(k, 0), AF_h[:, k, :], True, False)
                    mm(bank(b), mat(k, 1), AF_h[:, 8 + k, :], False, True)
                    mm(bank(b + 1), mat(k, 2), AF_h[:, k, :], True, False)
                    last = mm(bank(b + 1), mat(k, 0), AF_h[:, 8 + k, :], False, True)
                last.then_inc(sem("z_product"), 1)

            def inverse(o, idx):
                q = 11 * o + idx
                k = CLS_ORDER[idx] if idx < NCLS else idx
                wr, wi = wbuf[:, q % 2, 0, :], wbuf[:, q % 2, 1, :]
                pe.wait_ge(sem("w_ready"), q + 1)
                if k < NCLS:
                    n = NCLS * o + idx
                    b = 4 + 2 * (n % 2)
                    if n >= 2:
                        pe.wait_ge(sem("inverse_copied"), n - 1)
                    mm(bank(b), mat(k, 3), wr, True, False)
                    last = mm(bank(b), mat(k, 5), wi, False, True)
                    if k not in (0, 8):
                        mm(bank(b + 1), mat(k, 4), wr, True, False)
                        last = mm(bank(b + 1), mat(k, 3), wi, False, True)
                else:
                    b = 6 - 2 * o
                    pe.wait_ge(sem("inverse_copied"), NCLS * o + 8)
                    mm(bank(b), mat(k, 3), wr, k == NCLS, False)
                    last = mm(bank(b), mat(k, 5), wi, False, k == NCLS + 1)
                last.then_inc(sem("inverse_product"), 1)

            pe.wait_ge(sem("tokens_copied"), 3 * FEATS)
            for o in range(2):
                forward(o, 0)
                for idx in range(NCLS + CCLS):
                    if idx + 1 < NCLS + CCLS:
                        forward(o, idx + 1)
                    inverse(o, idx)

            pe.wait_ge(sem("hyena_done"), 1)
            for s in range(10):
                b = 3 * (s % 2)
                pe.wait_ge(sem("split_ready"), s + 1)
                if s >= 2:
                    pe.wait_ge(sem("qk_copied"), s - 1)
                if s != 8:
                    for h in range(HEADS):
                        turn(bank(b + h // 4, P, at=P * (h % 4)),
                             q_split[:, s % 2, h, :, :].rearrange("p s d -> p (s d)").bitcast(F32))
                for a in range(4):
                    last = turn(bank(b + 2, P, at=P * a),
                                k_split[:, s % 2, a // 2, a % 2, :, :].rearrange("p c d -> p (c d)").bitcast(F32))
                last.then_inc(sem("qk_transposed"), 1)

            def scores(i):
                h, t = ATT[i]
                v = h // GQA
                pieces = ((0, 512), (512, 1024), (1024, 1152)) if t < NLAT else ((1152, 1280),)
                if i:
                    pe.wait_ge(sem("exp_ready"), i)
                for s in range(2):
                    for a, (k0, k1) in enumerate(pieces):
                        last = mm(bank(a, k1 - k0), qT[:, h, P * t:P * (t + 1)], kT[:, s, v, k0:k1], s == 0, s == 1)
                last.then_inc(sem("scores_ready"), 1)

            def turn_probs(i):
                n = NTILE if ATT[i][1] < NLAT else 1
                pe.wait_ge(sem("exp_ready"), i + 1)
                if i:
                    pe.wait_ge(sem("probsT_a"), i)
                    pe.wait_ge(sem("probsT_d"), i)
                for k in range(n):
                    last = turn(PS[:, 1536 + P * k:1536 + P * (k + 1)], probs[:, i % 2, P * k:P * (k + 1)])
                last.then_inc(sem("probs_transposed"), 1)

            def values(i):
                h, t = ATT[i]
                pe.wait_ge(sem("probsT_a"), i + 1)
                pe.wait_ge(sem("probsT_d"), i + 1)
                if i >= 2:
                    pe.wait_ge(sem("attn_out"), i - 1)
                tiles = [*range(NLAT), None] if t < NLAT else [NLAT]
                for a, k in enumerate(tiles):
                    v = cache_v if k is None else qkv[:, k, (HEADS + KV) * HD:QKVW]
                    last = mm(bank(6 + i % 2, P), probsT[:, i % 2, a, :], v, a == 0, a == len(tiles) - 1)
                last.then_inc(sem("attn_product"), 1)

            pe.wait_ge(sem("qk_copied"), 10)
            scores(0)
            for i in range(len(ATT)):
                if i + 1 < len(ATT):
                    scores(i + 1)
                turn_probs(i)
                if i:
                    values(i - 1)
            values(len(ATT) - 1)

            def turn_mix(t):
                pe.wait_ge(sem("mix_normed"), t + 1)
                if t:
                    pe.wait_ge(sem("mixT_a"), t)
                    pe.wait_ge(sem("mixT_d"), t)
                for k in range(KT):
                    src = (attn if k < 4 else U[0])[:, t, P * (k % 4):P * (k % 4 + 1)]
                    last = turn(bank(k // 4, P, at=P * (k % 4)), src)
                last.then_inc(sem("mix_transposed"), 1)

            def project_mix(t):
                pe.wait_ge(sem("mixT_a"), t + 1)
                pe.wait_ge(sem("mixT_d"), t + 1)
                if t >= 2:
                    pe.wait_ge(sem("resid_ready"), t - 1)
                for c in range(2):
                    for k in range(KT):
                        last = mm(bank(4 + 2 * (t % 2) + c), mixT[:, t % 2, k, :], w_out[:, k, 512 * c:512 * (c + 1)],
                                  k == 0, k == KT - 1)
                last.then_inc(sem("mix_product"), 1)

            def route(t):
                pe.wait_ge(sem("h2_ready"), t + 1)
                if t:
                    pe.wait_ge(sem("logits_ready"), t)
                for k in range(KT):
                    last = turn(bank(2 + k // 4, P, at=P * (k % 4)), h2buf[:, t % 2, P * k:P * (k + 1)])
                last.then_inc(sem("h2T_product"), 1)
                pe.wait_ge(sem("h2T_ready"), t + 1)
                for k in range(KT):
                    last = mm(bank(2, ROUTE_W), h2Tt[:, k, :], route_w[:, k, :], k == 0, k == KT - 1)
                last.then_inc(sem("logit_product"), 1)

            pe.wait_ge(sem("attn_out"), len(ATT))
            turn_mix(0)
            pe.wait_ge(sem("w_out_loaded"), 16)
            pe.wait_ge(sem("route_w_loaded"), 16)
            for t in range(NTILE + 2):
                if t + 1 < NTILE:
                    turn_mix(t + 1)
                if t < NTILE:
                    project_mix(t)
                if t >= 2:
                    route(t - 2)

            pe.wait_ge(sem("assigned"), 1)
            flat = "p t n -> p (t n)"
            mm(bank(0, NTILE * NEXP), upper, r_all[:, :, :].rearrange(flat), True, False)
            mm(bank(0, NTILE * NEXP), ones, r_before[:, 0:NTILE, :].rearrange(flat), False, True)
            mm(bank(1, NEXP), ones, r_before[:, NTILE, :]).then_inc(sem("rank_product"), 1)
            for i in range(2 * NTILE):
                pe.wait_ge(sem("hot_ready"), i + 1)
                mm(bank(4, MAX_BLOCKS), r_hot[:, i % 2, :], r_tok[:, i % 2, :], i == 0, i == 2 * NTILE - 1).then_inc(
                    sem("slot_product"), 1)

            pe.sem_inc(sem("x_transposed"), 2)
            pe.sem_inc(sem("block_done"), 2)
            pe.sem_inc(sem("gate_up_product"), 2)
            pe.wait_ge(sem("route_done"), 1)
            pairs = pe.value_load(control[0:1, 60:61], min_val=1, max_val=MAX_BLOCKS // 2)
            with pe.Fori(0, pairs) as i:
                for u in range(2):
                    pe.wait_ge(sem(f"xg_loaded{u}"), 16 * i + 16)
                    pe.wait_ge(sem("y_a"), 2 * i + u + 1)
                    pe.wait_ge(sem("y_d"), 2 * i + u + 1)
                    for k in range(KT):
                        last = turn(bank(2 * u + k // 4, P, at=P * (k % 4)), xg[:, u, k:D:KT])
                    last.then_inc(sem("x_transposed"), 1)
                for u in range(2):
                    pe.wait_ge(sem("xT_ready"), 2 * i + u + 1)
                    pe.wait_ge(sem(f"we_loaded{u}"), 32 * i + 32)
                    for g in range(2):
                        for s in range(2):
                            for k in range(KT):
                                last = mm(bank(4 + u, P, at=256 * g + P * s), w_gu[:, u, g, k, s:FF:2], xgT[:, u, k, :],
                                          k == 0, k == KT - 1)
                    last.then_inc(sem("gate_up_product"), 1)
                for u in range(2):
                    pe.wait_ge(sem(f"wd_loaded{u}"), 16 * i + 16)
                    pe.wait_ge(sem("hidden_ready"), 2 * i + u + 1)
                    for c in range(2):
                        for s in range(2):
                            last = mm(bank((6, 2)[u] + c), hT[:, u, s, :], w_dn[:, u, s, 512 * c:512 * (c + 1)], s == 0, s == 1)
                    last.then_inc(sem("block_done"), 1)

        @block.vector
        def _(dve):
            steps = [0]

            def own(ins):
                steps[0] += 1
                ins.then_inc(sem("dve_step"), 1)
                dve.wait_ge(sem("dve_step"), steps[0])

            counts = {}

            def give(ins, name):
                counts[name] = counts.get(name, 0) + 1
                ins.then_inc(sem(name), 1)
                dve.wait_ge(sem(name), counts[name])

            def tt(out, a, b, op):
                return dve.tensor_tensor(out, a, b, op)

            def add(out, a, b):
                own(tt(out, a, b, ALU.add))

            def sub(out, a, b):
                own(tt(out, a, b, ALU.subtract))

            def scaled(out, a, s):
                own(dve.tensor_scalar(out, a, s, None, ALU.mult))

            def axpy(out, a, s, b, op=ALU.add):
                own(dve.scalar_tensor_tensor(out, a, s, b, ALU.mult, op))

            def rsqrt(out, v, tmp):
                own(dve.tensor_scalar(out.bitcast(I32), v.bitcast(I32), -0.5, RSQRT_SEED, ALU.mult, ALU.add))
                for _ in range(4):
                    own(tt(tmp, out, out, ALU.mult))
                    own(tt(tmp, tmp, v, ALU.mult))
                    own(dve.tensor_scalar(tmp, tmp, -0.5, 1.5, ALU.mult, ALU.add))
                    own(tt(out, out, tmp, ALU.mult))

            def transform_tiles(A, W, X, name):
                own(tt(W[:, 0:4, :], X[:, 0:4, :], X[:, 4:8, :], ALU.add))
                own(tt(W[:, 4:8, :], X[:, 0:4, :], X[:, 4:8, :], ALU.subtract))
                w = [W[:, i, :] for i in range(10)]
                a = [A[:, i, :] for i in range(16)]
                x = [X[:, j, :] for j in range(8)]
                add(w[8], w[0], w[2])
                add(w[9], w[1], w[3])
                add(a[0], w[8], w[9])
                sub(a[8], w[8], w[9])
                sub(a[4], w[0], w[2])
                give(tt(a[12], w[3], w[1], ALU.subtract), name)
                sub(w[8], w[5], w[7])
                add(w[9], w[5], w[7])
                axpy(a[2], w[8], C2, w[4])
                axpy(a[6], w[8], -C2, w[4])
                axpy(a[10], w[9], -C2, w[6], ALU.subtract)
                give(dve.scalar_tensor_tensor(a[14], w[9], -C2, w[6], ALU.mult, ALU.add), name)
                own(tt(W[:, 0:3, :], X[:, 1:4, :], X[:, 7:4:-1, :], ALU.subtract))
                own(tt(W[:, 3:6, :], X[:, 1:4, :], X[:, 7:4:-1, :], ALU.add))
                axpy(w[6], w[1], C2, x[0])
                axpy(w[7], w[1], -C2, x[0])
                scaled(w[8], w[2], C3)
                axpy(w[8], w[0], C1, w[8])
                scaled(w[9], w[2], C1)
                axpy(w[9], w[0], C3, w[9], ALU.subtract)
                add(a[1], w[6], w[8])
                sub(a[7], w[6], w[8])
                add(a[3], w[7], w[9])
                sub(a[5], w[7], w[9])
                axpy(w[6], w[4], C2, x[4])
                axpy(w[7], w[4], C2, x[4], ALU.subtract)
                scaled(w[8], w[5], C1)
                axpy(w[8], w[3], C3, w[8])
                scaled(w[9], w[5], C3)
                axpy(w[9], w[3], C1, w[9], ALU.subtract)
                axpy(a[9], w[8], -1.0, w[6], ALU.subtract)
                sub(a[15], w[6], w[8])
                axpy(a[11], w[9], -1.0, w[7], ALU.subtract)
                give(tt(a[13], w[7], w[9], ALU.subtract), name)

            def combine_tiles(A, W, gate, z):
                w = [W[:, i, :] for i in range(10)]
                a = [A[:, i, :] for i in range(16)]
                add(w[0], a[0], a[8])
                sub(w[1], a[0], a[8])
                add(a[0], w[0], a[4])
                sub(a[8], w[0], a[4])
                sub(w[0], w[1], a[12])
                add(a[4], w[1], a[12])
                add(w[1], a[2], a[6])
                sub(w[2], a[14], a[10])
                sub(w[3], a[2], a[6])
                add(a[2], a[10], a[14])
                sub(a[6], w[3], a[2])
                add(a[10], w[3], a[2])
                add(a[2], a[0], w[1])
                sub(a[14], a[0], w[1])
                add(a[0], a[8], w[2])
                sub(a[12], a[8], w[2])
                axpy(a[8], a[6], C2, w[0])
                axpy(w[1], a[6], -C2, w[0])
                axpy(w[2], a[10], -C2, a[4])
                axpy(w[3], a[10], C2, a[4])
                add(w[4], a[1], a[7])
                sub(w[5], a[1], a[7])
                add(w[6], a[3], a[5])
                sub(w[7], a[3], a[5])
                add(a[1], a[9], a[15])
                sub(a[7], a[9], a[15])
                add(a[3], a[11], a[13])
                sub(a[5], a[11], a[13])
                add(w[8], w[4], w[6])
                sub(w[9], w[4], w[6])
                scaled(w[4], w[5], C1)
                axpy(w[4], w[7], C3, w[4])
                scaled(w[6], w[5], C3)
                axpy(w[6], w[7], -C1, w[6])
                scaled(a[9], a[1], C3)
                axpy(a[9], a[3], C1, a[9])
                scaled(a[11], a[1], C1)
                axpy(a[11], a[3], -C3, a[11])
                add(a[13], a[7], a[5])
                sub(a[15], a[7], a[5])
                add(a[1], a[2], w[8])
                sub(a[3], a[14], a[15])
                sub(w[0], w[9], a[13])
                add(w[5], w[9], a[13])
                axpy(a[5], w[0], C2, a[0])
                axpy(a[7], w[5], -C2, a[12])
                sub(w[7], w[4], a[9])
                add(w[9], w[4], a[9])
                add(a[4], a[8], w[7])
                sub(a[6], w[3], w[9])
                sub(w[7], w[6], a[11])
                add(w[9], w[6], a[11])
                add(a[9], w[2], w[7])
                sub(a[10], w[1], w[9])
                for j, y in enumerate((a[1], a[4], a[5], a[9], a[3], a[10], a[7], a[6])):
                    own(tt(z[:, j, :], gate[:, j, :], y, ALU.mult))

            dve.wait_ge(sem("small_loaded"), 16 * 8)
            freq = hid_cols[0:HID, HID + 2:HID + 3]
            for layer in range(2):
                own(tt(hid_cols[0:HID, HID + 3 + layer:HID + 4 + layer], hid_cols[0:HID, HID + layer:HID + layer + 1], freq, ALU.mult))
            for layer in range(2):
                dve.wait_ge(sem("hidden_product"), layer + 1)
                own(dve.tensor_scalar(arg, PS[0:HID, 0:T], freq, hid_cols[0:HID, HID + 3 + layer:HID + 4 + layer], ALU.mult, ALU.add))
                own(dve.tensor_scalar(turns, arg, float(1 / (2 * np.pi)), ROUND_MAGIC, ALU.mult, ALU.add))
                own(dve.tensor_scalar(turns, turns, -ROUND_MAGIC, None, ALU.add))
                axpy(arg, turns, -TWO_PI_HI, arg)
                axpy(arg, turns, -TWO_PI_LO, arg)
                give(dve.tensor_scalar(arg, arg, PI_BELOW, -PI_BELOW, ALU.min, ALU.max), "arg_ready")

            for o in range(2):
                if o:
                    dve.wait_ge(sem("square_ready"), 18)
                    dve.wait_ge(sem("spectrum_product"), 22)
                for n, j, d in filter_items(o):
                    dve.wait_ge(sem("taps_product"), n + 1)
                    dve.wait_ge(sem("window_ready"), n + 1)
                    taps_out = tt(hbuf[:, d, j, :], bank(3 + n % 2), win[:, n % 4, :], ALU.mult)
                    if d == 1 and j in (0, NLAT):
                        own(taps_out)
                        taps_out = dve.memset(hbuf[0:1, d, j, :], 0.0)
                    give(taps_out, "taps_ready")
                dve.wait_ge(sem("norm_product"), 18 * (o + 1))
                own(dve.tensor_copy(norms[:, 0, :], bank(5)))
                give(dve.tensor_copy(norms[:, 1, :], bank(6)), "norms_ready")
                dve.wait_ge(sem("norm_col"), o + 1)
                own(dve.tensor_scalar(col_v, bank(7, 8), EPS, None, ALU.add))
                rsqrt(col_r[:, o, :], col_v, col_t)
                own(tt(col_s, col_v, col_r[:, o, :], ALU.mult))
                own(tt(col_s[:, 0:4], col_s[:, 0:4], skip_col[:, o, :], ALU.mult))
                give(tt(col_s[:, 4:8], col_s[:, 4:8], skip_col[:, o, :], ALU.mult), "skip_scaled")
                dve.wait_ge(sem("skip_row"), o + 1)
                own(tt(hbuf[0:1, 0, 0, :], hbuf[0:1, 0, 0, :], bank(7, rows=1), ALU.add))
                give(tt(hbuf[0:1, 0, NLAT, :], hbuf[0:1, 0, NLAT, :], bank(6, rows=1), ALU.add), "skip_added")
                dve.wait_ge(sem("square_ready"), 18 * (o + 1))
                add(hbuf[:, 0, :, :], hbuf[:, 0, :, :], hbuf[:, 1, :, :])
                axpy(hbuf[:, 1, :, :], hbuf[:, 1, :, :], -2.0, hbuf[:, 0, :, :])
                transform_tiles(AF_f, TT_f, hbuf[:, 0, 0:NLAT, :], "tiles_transformed")
                dve.wait_ge(sem("spectrum_product"), 22 * o + 11)
                transform_tiles(AF_f, TT_f, hbuf[:, 1, 0:NLAT, :], "tiles_transformed")

            dve.wait_ge(sem("mod_col_loaded"), 64)
            own(tt(mod_col[:, :, :, :], mod_col[:, :, :, :],
                   bmod_col.unsqueeze(1).broadcast_to([P, 2, 2, KT]), ALU.add))
            own(dve.tensor_scalar(mod_col[:, :, 1, :], mod_col[:, :, 1, :], 1.0, None, ALU.add))
            dve.wait_ge(sem("x_loaded"), 16)
            for k in range(KT):
                for c, (t0, t1) in enumerate(((0, LAT), (LAT, T))):
                    ins = dve.tensor_scalar(xT[:, k, t0:t1], xT[:, k, t0:t1], mod_col[:, c, 1, k:k + 1], mod_col[:, c, 0, k:k + 1],
                                            ALU.mult, ALU.add)
                    own(ins) if (k, c) != (KT - 1, 1) else give(ins, "hT_ready")

            for lc in range(2):
                own(dve.tensor_copy(tap_s[:, 0:4, lc, 0:3], taps[:, 0:4, :]))
                own(dve.tensor_copy(tap_s[:, 0:4, lc, 3], tap_bias[:, 0:4]))
                for o in range(2):
                    f = slice(4 * o + 4, 4 * o + 8)
                    r = col_r[:, o, 4 * lc:4 * lc + 4]
                    own(tt(tap_s[:, f, lc, 0:3], taps[:, f, :], r.unsqueeze(2).broadcast_to([P, 4, 3]), ALU.mult))
                    own(tt(tap_s[:, f, lc, 3], tap_bias[:, f], r, ALU.mult))
            for r in range(3):
                dve.wait_ge(rs["spec"][r], SPEC_STORED[r])
            for f in range(FEATS):
                ps0 = 1536 * (f % 2)
                dve.wait_ge(sem("feature_product"), f + 1)
                if f >= 2:
                    dve.wait_ge(sem("tokens_product"), 3 * (f - 1))
                out = uc[:, f % 2, :]
                for lc, (t0, t1) in enumerate(((0, LAT), (LAT, T))):
                    w = [tap_s[:, f, lc, i:i + 1] for i in range(4)]
                    own(dve.tensor_scalar(out[:, t0:t1], PS[:, ps0 + t0:ps0 + t1], w[1], w[3], ALU.mult, ALU.add))
                    axpy(out[:, t0 + 1:t1], PS[:, ps0 + t0:ps0 + t1 - 1], w[0], out[:, t0 + 1:t1])
                    ins = dve.scalar_tensor_tensor(out[:, t0:t1 - 1], PS[:, ps0 + t0 + 1:ps0 + t1], w[2], out[:, t0:t1 - 1],
                                                   ALU.mult, ALU.add)
                    own(ins) if lc == 0 else give(ins, "conv_ready")

            dve.wait_ge(sem("slots_zeroed"), 16 * 5)
            dve.wait_ge(sem("tokens_copied"), 3 * FEATS)
            for o in range(2):
                transform_tiles(AF_h, TT_h, U[0][:, 0:NLAT, :], "z_transformed")
                for idx in range(NCLS + CCLS):
                    q = 11 * o + idx
                    dve.wait_ge(sem("z_product"), q + 1)
                    dve.wait_ge(sem(f"g_loaded{q % 2}"), 16 * (q // 2 + 1))
                    b = 2 * (q % 2)
                    z = PS[:, 512 * b:512 * (b + 2)].rearrange("p (i c) -> p i c", i=2)
                    own(tt(prod[:, 0:2, :], z, gbuf[:, q % 2, :, :], ALU.mult))
                    own(tt(prod[:, 2:4, :], z, gbuf[:, q % 2, ::-1, :], ALU.mult))
                    if q >= 2:
                        dve.wait_ge(sem("inverse_product"), q - 1)
                    sub(wbuf[:, q % 2, 0, :], prod[:, 0, :], prod[:, 1, :])
                    give(tt(wbuf[:, q % 2, 1, :], prod[:, 2, :], prod[:, 3, :], ALU.add), "w_ready")
                dve.wait_ge(sem("inverse_product"), 11 * (o + 1))
                own(tt(U[0][:, NLAT, :], U[o + 1][:, NLAT, :], bank(6 - 2 * o), ALU.mult))
                dve.wait_ge(sem("inverse_copied"), NCLS * (o + 1))
                combine_tiles(AF_h, TT_h, U[o + 1], U[0])
            dve.sem_inc(sem("hyena_done"), 1)

            scaled(qk_gain[:, 0:HEADS * HD], qk_gain[:, 0:HEADS * HD], HD ** -0.5)
            for t in range(NTILE):
                dve.wait_ge(sem("qk_squared"), t + 1)
                give(dve.tensor_reduce(ss_qk[:, 10 * t:10 * t + 10], probs[:, t % 2, 0:640].rearrange("p (h d) -> p h d", h=10),
                                       AX.X, ALU.add), "qk_summed")
            own(dve.tensor_scalar(ss_qk, ss_qk, 1.0 / HD, EPS, ALU.mult, ALU.add))
            rsqrt(rstd_qk, ss_qk, ss_tmp)
            dve.wait_ge(sem("cache_loaded"), 48)
            dve.wait_ge(sem("gains_loaded"), 32)
            heads = "p (h d) -> p h d"
            for s in range(10):
                tile = s if s < 8 else NLAT
                x = qkv[:, tile, 0:640]
                xh = x.rearrange(heads, h=10)
                if s != 8:
                    own(tt(xh, xh, rstd_qk[:, 10 * tile:10 * tile + 10].unsqueeze(2).broadcast_to([P, 10, HD]), ALU.mult))
                    own(tt(x, x, qk_gain, ALU.mult))
                if s < 8:
                    c = rot[:, s, 0, :].unsqueeze(1).broadcast_to([P, 10, HD])
                    own(tt(qk_work.rearrange(heads, h=10), xh, c, ALU.mult))
                    swap = probs[:, 0, 0:640]
                    quarters = "p (h a s f) -> p h a s f"
                    x5, s5 = (v.rearrange(quarters, h=10, a=2, s=2) for v in (x, swap))
                    sin = rot[:, s, 1, :].rearrange("p (a s f) -> p a s f", a=2, s=2)
                    for half in range(2):
                        own(tt(s5[:, :, :, half, :], x5[:, :, :, 1 - half, :],
                               sin[:, :, half, :].unsqueeze(1).broadcast_to([P, 10, 2, 16]), ALU.mult))
                    own(tt(x, qk_work, swap, ALU.add))
                if s >= 2:
                    dve.wait_ge(sem("qk_transposed"), s - 1)
                r = s % 2
                if s != 8:
                    q = x[:, 0:HEADS * HD].rearrange(heads, h=HEADS)
                    own(dve.tensor_copy(q_split[:, r, :, 0, :], q))
                    own(tt(q_split[:, r, :, 1, :], q, q_split[:, r, :, 0, :].bitcast(F32), ALU.subtract))
                k = (cache_k if s == 8 else x[:, HEADS * HD:]).rearrange(heads, h=KV)
                for v in range(KV):
                    kk = k[:, v, :].unsqueeze(1).broadcast_to([P, 2, HD])
                    own(dve.tensor_copy(k_split[:, r, 0, v, :, :], kk))
                    ins = tt(k_split[:, r, 1, v, :, :], kk, k_split[:, r, 0, v, :, :].bitcast(F32), ALU.subtract)
                    own(ins) if v == 0 else give(ins, "split_ready")

            def maximum(i):
                n = NTILE * P if ATT[i][1] < NLAT else P
                dve.wait_ge(sem("scores_ready"), i + 1)
                give(dve.tensor_reduce(nmax[:, i:i + 1], PS[:, 0:n], AX.X, ALU.max, negate=True), "max_ready")

            def weighted(i):
                h, t = ATT[i]
                dve.wait_ge(sem("attn_product"), i + 1)
                own(dve.reciprocal(precip[:, i:i + 1], psums[:, i:i + 1]))
                v = HD * (h // GQA)
                give(dve.tensor_scalar(attn[:, t, HD * h:HD * (h + 1)], bank(6 + i % 2, HD, at=v), precip[:, i:i + 1], None,
                                       ALU.mult), "attn_out")

            maximum(0)
            for i in range(len(ATT)):
                if i + 1 < len(ATT):
                    maximum(i + 1)
                dve.wait_ge(sem("probs_transposed"), i + 1)
                if i >= 2:
                    dve.wait_ge(sem("attn_product"), i - 1)
                if ATT[i][1] < NLAT:
                    give(dve.tensor_copy(probsT[:, i % 2, 4:9, :], PS[:, 2048:2688].rearrange("p (t n) -> p t n", t=5)), "probsT_d")
                else:
                    give(dve.tensor_copy(bn[:, 0:1], ones[:, 0:1]), "probsT_d")
                if i:
                    weighted(i - 1)
            weighted(len(ATT) - 1)

            for n in range(2 * NTILE):
                dve.wait_ge(sem("mix_squared"), n + 1)
                give(dve.tensor_reduce(stat[:, 0, 8 * n:8 * n + 8], h2buf[:, n % 2, 0:HW].rearrange("p (g d) -> p g d", g=8),
                                       AX.X, ALU.add), "mix_summed")
            own(dve.tensor_scalar(stat[:, 0, :], stat[:, 0, :], 1.0 / HD, EPS, ALU.mult, ALU.add))
            rsqrt(stat[:, 1, :], stat[:, 0, :], stat[:, 2, :])
            for n in range(2 * NTILE):
                t, src = divmod(n, 2)
                x = (attn, U[0])[src][:, t, :].rearrange("p (g d) -> p g d", g=8)
                ins = tt(x, x, stat[:, 1, 8 * n:8 * n + 8].unsqueeze(2).broadcast_to([P, 8, HD]), ALU.mult)
                own(ins) if src == 0 else give(ins, "mix_normed")

            def gain_half(t):
                dve.wait_ge(sem("mix_transposed"), t + 1)
                if t >= 2:
                    dve.wait_ge(sem("mix_product"), t - 1)
                for k in range(4, 8):
                    ins = dve.tensor_scalar(mixT[:, t % 2, k, :], bank(1, P, at=P * (k - 4)), out_gain[:, k:k + 1], None, ALU.mult)
                    own(ins) if k < 7 else give(ins, "mixT_d")

            def normalized(out, x, tmp):
                for c in range(2):
                    own(dve.bn_stats(bn[:, 6 * c:6 * c + 6], x[:, 512 * c:512 * (c + 1)]))
                own(dve.bn_aggr(bn[:, 12:14], bn[:, 0:12]))
                own(dve.tensor_scalar(bn[:, 13:14], bn[:, 13:14], EPS, None, ALU.add))
                rsqrt(bn[:, 14:15], bn[:, 13:14], bn[:, 15:16])
                return dve.tensor_scalar(out, x, bn[:, 12:13], bn[:, 14:15], ALU.subtract, ALU.mult)

            def first_norm(t):
                dve.wait_ge(sem("mix_product"), t + 1)
                b = 4 + 2 * (t % 2)
                own(tt(resid, PS[:, 512 * b:512 * (b + 2)], rows[:, 4 * (t == NLAT) + 2, :], ALU.mult))
                dve.wait_ge(sem(f"xres_loaded{t % 2}"), 16 * (t // 2 + 1))
                give(dve.scalar_tensor_tensor(resid, xres[:, t % 2, :], ALPHA, resid, ALU.mult, ALU.add), "resid_ready")
                if t:
                    dve.wait_ge(sem("h2_ready"), t)
                give(normalized(xnorm, resid, None), "xnorm_ready")

            def take_logits(t):
                dve.wait_ge(sem("logit_product"), t + 1)
                give(tt(logits[:, t, :], bank(2, ROUTE_W), route_bias, ALU.add), "logits_ready")

            dve.wait_ge(sem("rows_ready"), 1)
            gain_half(0)
            for t in range(NTILE + 3):
                if t + 1 < NTILE:
                    gain_half(t + 1)
                if 1 <= t <= NTILE:
                    first_norm(t - 1)
                if t >= 3:
                    take_logits(t - 3)

            def first_largest(out, values, largest, eq, least, n):
                wide = [P, NTILE, n]
                own(tt(eq, values, largest.unsqueeze(2).broadcast_to(wide), ALU.is_equal))
                axpy(eq, eq, -64.0, row128[:, 0:n].unsqueeze(1).broadcast_to(wide))
                own(dve.tensor_reduce(least, eq, AX.X, ALU.min))
                own(tt(out, eq, least.unsqueeze(2).broadcast_to(wide), ALU.is_equal))

            groups = logits[:, :, 0:NGRP]
            experts = logits[:, :, NGRP:].rearrange("p t (g e) -> p t g e", g=NGRP)
            own(dve.tensor_reduce(r_max, groups, AX.X, ALU.max))
            give(tt(r_g, groups, r_max.unsqueeze(2).broadcast_to([P, NTILE, NGRP]), ALU.subtract), "group_shifted")
            dve.wait_ge(sem("group_exp"), 1)
            own(dve.tensor_reduce(r_pg, r_exp, AX.X, ALU.add))
            own(dve.reciprocal(r_pg, r_pg))
            first_largest(r_g, groups, r_max, r_eq, r_min, NGRP)
            own(tt(r_prod, experts, r_g.unsqueeze(3).broadcast_to([P, NTILE, NGRP, EPG]), ALU.mult))
            own(dve.tensor_reduce(r_sel, r_prod.rearrange("p t g e -> p t e g"), AX.X, ALU.add))
            for c in range(2):
                own(dve.tensor_reduce(r_v[:, c, :], r_sel, AX.X, ALU.max))
                first_largest(r_pick[:, c, :, :], r_sel, r_v[:, c, :], r_cand, r_min, EPG)
                if c == 0:
                    axpy(r_sel, r_pick[:, 0, :, :], -BIG, r_sel)
            give(tt(r_d, r_v[:, 1, :], r_v[:, 0, :], ALU.subtract), "pair_shifted")
            dve.wait_ge(sem("pair_exp"), 1)
            own(dve.tensor_scalar(r_max, r_d, 1.0, None, ALU.add))
            own(dve.reciprocal(r_max, r_max))
            own(tt(mix_w[:, 0, :], r_pg, r_max, ALU.mult))
            own(tt(mix_w[:, 1, :], mix_w[:, 0, :], r_d, ALU.mult))
            four = [P, NTILE, NGRP, EPG]
            for c in range(2):
                own(tt(r_mask[:, c, :, :].rearrange("p t (g e) -> p t g e", g=NGRP), r_g.unsqueeze(3).broadcast_to(four),
                       r_pick[:, c, :, :].unsqueeze(2).broadcast_to(four), ALU.mult))
            own(tt(r_all, r_mask[:, 0, :, :], r_mask[:, 1, :, :], ALU.add))
            own(dve.memset(r_before[:, 0, :], 0.0))
            for t in range(NTILE):
                ins = tt(r_before[:, t + 1, :], r_before[:, t, :], r_all[:, t, :], ALU.add)
                own(ins) if t + 1 < NTILE else give(ins, "assigned")
            dve.wait_ge(sem("rank_product"), 1)
            own(dve.tensor_copy(r_count, bank(1, NEXP)))
            own(dve.tensor_scalar(r_blocks, r_count, 0.0, None, ALU.is_gt))
            for m in range(1, NTILE):
                own(dve.scalar_tensor_tensor(r_blocks, r_count, float(P * m), r_blocks, ALU.is_gt, ALU.add))
            own(dve.tensor_copy(r_scan[:, 0, :], r_blocks))
            for i in range(5):
                src, dst, step = r_scan[:, i % 2, :], r_scan[:, (i + 1) % 2, :], 1 << i
                own(dve.tensor_copy(dst[:, 0:step], src[:, 0:step]))
                own(tt(dst[:, step:], src[:, step:], src[:, 0:NEXP - step], ALU.add))
            ends = r_scan[:, 1, :]
            sub(r_base, ends, r_blocks)
            scaled(r_base, r_base, float(P))
            own(tt(r_slot, bank(0, NTILE * NEXP).rearrange("p (t n) -> p t n", t=NTILE),
                   r_base.unsqueeze(1).broadcast_to([P, NTILE, NEXP]), ALU.add))
            for c in range(2):
                own(tt(r_mask[:, c, :, :], r_mask[:, c, :, :], r_slot, ALU.mult))
                own(dve.tensor_reduce(r_pos[:, NTILE * c:NTILE * (c + 1)], r_mask[:, c, :, :], AX.X, ALU.add))
            own(dve.tensor_copy(slot_of, r_pos))
            n = 2 * NTILE
            own(dve.tensor_scalar(r_int[:, 0:n], slot_of, P - 1, None, ALU.bitwise_and))
            own(dve.tensor_scalar(r_int[:, n:2 * n], slot_of, 7, None, ALU.logical_shift_right))
            own(dve.tensor_copy(r_rowblk.rearrange("p a n -> p (a n)"), r_int))
            for i in range(n):
                if i >= 2:
                    dve.wait_ge(sem("slot_product"), i - 1)
                own(dve.tensor_scalar(r_hot[:, i % 2, :], row128, r_rowblk[:, 0, i:i + 1], None, ALU.is_equal))
                t = i % NTILE
                give(dve.tensor_scalar(r_tok[:, i % 2, :], row128[:, 0:MAX_BLOCKS], r_rowblk[:, 1, i:i + 1],
                                       token_no[:, t:t + 1], ALU.is_equal, ALU.mult), "hot_ready")
            blocks_first = [P, MAX_BLOCKS, NEXP]
            own(tt(r_cmp, ends.unsqueeze(1).broadcast_to(blocks_first),
                   row128[:, 0:MAX_BLOCKS].unsqueeze(2).broadcast_to(blocks_first), ALU.is_le))
            own(dve.tensor_reduce(r_eid[:, 0:MAX_BLOCKS], r_cmp, AX.X, ALU.add))
            own(dve.tensor_scalar(r_eid[:, 0:MAX_BLOCKS], r_eid[:, 0:MAX_BLOCKS], float(NEXP - 1), None, ALU.min))
            own(dve.tensor_copy(control[:, 0:MAX_BLOCKS], r_eid[0:1, 0:MAX_BLOCKS]))
            own(dve.tensor_scalar(r_eid[:, 60:61], ends[:, NEXP - 1:NEXP], 1.0, None, ALU.add))
            own(dve.tensor_copy(control[:, 61:62], r_eid[0:1, 60:61]))
            own(dve.tensor_scalar(control[:, 60:61], control[:, 61:62], 1, None, ALU.logical_shift_right))
            dve.wait_ge(sem("slot_product"), n)
            give(dve.tensor_copy(slot_token, bank(4, MAX_BLOCKS)), "route_done")

            pairs = dve.value_load(control[0:1, 60:61], min_val=1, max_val=MAX_BLOCKS // 2)
            dve.sem_inc(sem("y_d"), 2)
            with dve.Fori(0, pairs) as i:
                for u in range(2):
                    dve.wait_ge(sem("x_transposed"), 2 * i + u + 3)
                    dve.tensor_copy(xgT[:, u, :, :], PS[:, 1024 * u:1024 * (u + 1)].rearrange("p (k n) -> p k n", k=KT)).then_inc(
                        sem("xT_ready"), 1)
                for u in range(2):
                    dve.wait_ge(sem("gate_ready"), 2 * i + u + 1)
                    tt(hT[:, u, :, :], gate_act[:, u, :, :], bank(4 + u, 256, at=256).rearrange("p (s n) -> p s n", s=2),
                       ALU.mult).then_inc(sem("hidden_ready"), 1)
                for u in range(2):
                    dve.wait_ge(sem("block_done"), 2 * i + u + 3)
                    dve.wait_ge(sem(f"slot_y_stored{u}"), 16 * i + 16)
                    dve.tensor_copy(ybuf[:, u, 512:1024], bank((7, 3)[u])).then_inc(sem("y_d"), 1)

            for t in range(NTILE):
                y, g2 = yg[:, t % 2, :, :], rows[:, 4 * (t == NLAT) + 3, :]
                a = acc[:, t % 2, :]
                dve.wait_ge(sem(f"yg_loaded{t % 2}"), 32 * (t // 2 + 1))
                scaled(a, y[:, 0, :], mix_w[:, 0, t:t + 1])
                give(dve.scalar_tensor_tensor(a, y[:, 1, :], mix_w[:, 1, t:t + 1], a, ALU.mult, ALU.add), "acc_ready")
                own(tt(a, a, g2, ALU.mult))
                axpy(a, x1[:, t, :], ALPHA, a)
                if t >= 2:
                    dve.wait_ge(sem(f"y_stored{t % 2}"), 16 * (t // 2))
                give(normalized(ynorm[:, t % 2, :], a, None), "ynorm_ready")


def kernel(**inputs):
    import numpy as _np
    import concourse.bacc as _bacc
    from concourse import mybir as _mybir
    from concourse.bass_utils import run_bass_kernel_spmd as _run

    a = {k: _np.asarray(v) for k, v in inputs.items()}
    lay = _np.ascontiguousarray
    tok = _np.concatenate([a["x_sample"][0], a["x_prompt"][0]], 0)

    def columns(v):
        return v.reshape(-1, P).T

    cond = _np.stack([a["c"][0], a["c_ctx"]], 0).reshape(2, P, KT).transpose(1, 0, 2).reshape(P, 2 * KT)
    b_mod = a["b_mod"][0]
    arrays = {
        "cols": _np.concatenate([
            a["hy_short_w"][0].T.reshape(FEATS, P, 3).transpose(1, 0, 2).reshape(P, 3 * FEATS),
            columns(a["hy_short_b"][0]),
            columns(a["hy_skip"][0].reshape(-1)),
            columns(_np.concatenate([a["attn_out_gain"][0], a["hy_out_gain"][0]])),
            b_mod[0:D].reshape(P, KT), b_mod[D:2 * D].reshape(P, KT), cond], 1),
        "tables": small_tables(), "ntime": negative_times(), "feats": position_features(),
        "mats": fourier_matrices(), "rot": rotary_tables(),
        "hid": _np.concatenate([a["hy_f_w2"][0], a["hy_f_b1"][0][:, None], a["hy_f_b2"][0][:, None], a["hy_freq"][0][:, None]], 1),
        "hy_f_w1": a["hy_f_w1"][0], "hy_f_w3": a["hy_f_w3"][0], "hy_decay": a["hy_decay"][0],
        "qk_gain": _np.concatenate([a["q_gain"][0]] * HEADS + [a["k_gain"][0]] * KV),
        "route_bias": _np.concatenate([a["router_grp_b"][0], a["router_exp_b"][0]]),
        "route_w": _np.concatenate([a["router_grp_w"][0], a["router_exp_w"][0]], 1),
        "w_mod": a["w_mod"][0], "b_mod": b_mod, "w_in": a["w_in"][0], "w_out": a["w_out"][0],
        "xT": tok.T, "x_tok": tok,
        "cache_k": a["cache_k"][0, 0].reshape(P, KV * HD), "cache_v": a["cache_v"][0, 0].reshape(P, KV * HD),
        "ln1_g": a["ln1_g"][0], "ln1_b": a["ln1_b"][0], "ln2_g": a["ln2_g"][0], "ln2_b": a["ln2_b"][0],
        "exp_w_gate": a["exp_w_gate"][0], "exp_w_up": a["exp_w_up"][0], "exp_w_down": a["exp_w_down"][0],
    }
    arrays = {k: lay(v) for k, v in arrays.items()}
    nc = _bacc.Bacc("TRN2", target_bir_lowering=False, num_devices=1)
    I = {k: nc.dram_tensor("in_" + k, list(v.shape), _mybir.dt.from_np(v.dtype), kind="ExternalInput").ap()
         for k, v in arrays.items()}
    shapes = {"ctx": [CTX, D], "lat": [LAT, D], "new_k": [CTX, KV * HD], "new_v": [CTX, KV * HD]}
    O = {k: nc.dram_tensor("out_" + k, s, F32, kind="ExternalOutput").ap() for k, s in shapes.items()}
    build(nc, I, O)
    r = _run(nc, [{"in_" + k: v for k, v in arrays.items()}], core_ids=[0]).results[0]
    cache = (1, 1, CTX, KV, HD)
    return (r["out_ctx"].reshape(1, CTX, D), r["out_lat"].reshape(1, LAT, D),
            r["out_new_k"].reshape(cache), r["out_new_v"].reshape(cache))
```

```python
from contextlib import ExitStack

import concourse.bass as bass
import numpy as np
from concourse import mybir

ALU = mybir.AluOpType
ACT = mybir.ActivationFunctionType
AX = mybir.AxisListType
F32 = mybir.dt.float32
F32R = mybir.dt.float32r
I32 = mybir.dt.int32

P = 128
D = 1024
KT = D // P
LAT = 1024
CTX = 128
NLAT = LAT // P
NTILE = NLAT + 1
T = LAT + CTX
HEADS, KV, HD = 8, 2, 64
GQA = HEADS // KV
QKVW = (HEADS + 2 * KV) * HD
HW = 512
IN_W = QKVW + 3 * HW
CHUNK = 384
MOD_CHUNKS = 6 * D // CHUNK
IN_CHUNKS = IN_W // CHUNK
QKV_CHUNKS = QKVW // CHUNK
FEATS = 3 * HW // P
POS = 33
HID = 64
NEXP, EPG, NGRP = 32, 8, 4
FF = 256
ROUTE_W = NGRP + NEXP
MAX_BLOCKS = 50
ALPHA = 2.0 ** 0.25
EPS = 1e-6
NCLS = 9
CCLS = 2
C1, C2, C3 = (float(np.cos(np.pi * m / 8)) for m in (1, 2, 3))
ROUND_MAGIC = 12582912.0
TWO_PI_HI = 6.28125
TWO_PI_LO = float(2 * np.pi - 6.28125)
PI_BELOW = 3.1415925
RSQRT_SEED = float(0x5F3759DF)
BIG = 1e30

N_MATS = 6 * NCLS + 4 * CCLS


def fourier_matrices():
    p = np.arange(P, dtype=np.float64)[:, None]
    q = np.arange(P, dtype=np.float64)[None, :]
    mats = []
    for k1 in range(NCLS):
        ang = 2 * np.pi * ((p * (k1 + 16 * q)) % (2 * LAT)) / (2 * LAT)
        mats += [np.cos(ang), np.sin(ang), -np.sin(ang)]
        scale = (1.0 if k1 in (0, 8) else 2.0) / (2 * LAT)
        mats += [scale * np.cos(ang).T, scale * np.sin(ang).T, -scale * np.sin(ang).T]
    for k1 in range(CCLS):
        ang = 2 * np.pi * ((p * (k1 + 2 * q)) % (2 * CTX)) / (2 * CTX)
        mats += [np.cos(ang), -np.sin(ang), np.cos(ang).T / (2 * CTX), -np.sin(ang).T / (2 * CTX)]
    return np.ascontiguousarray(np.stack(mats, 1).astype(np.float32))


def position_features():
    cols = []
    for length in (LAT, CTX):
        t = np.arange(length, dtype=np.float64) / length
        ang = 2.0 * np.pi * t[None, :] * np.arange(1, 17)[:, None]
        cols.append(np.concatenate([t[None, :], np.sin(ang), np.cos(ang)], 0))
    return np.ascontiguousarray(np.concatenate(cols, 1).astype(np.float32))


def negative_times():
    t = np.arange(P, dtype=np.float64)[:, None]
    lat = -(t + P * np.arange(NLAT)[None, :]) / LAT
    return np.ascontiguousarray(np.concatenate([lat, -t / CTX], 1).astype(np.float32))


def rotary_tables():
    t = np.arange(LAT)
    inv = 10000.0 ** (-np.arange(16) / 16.0)
    ang = np.stack([(t // 64)[:, None] * inv, (t % 64)[:, None] * inv], 1)
    cos = np.stack([np.cos(ang)] * 2, 2).reshape(LAT, HD)
    sin = np.stack([-np.sin(ang), np.sin(ang)], 2).reshape(LAT, HD)
    both = np.stack([cos, sin], 1).reshape(NLAT, P, 2, HD).transpose(1, 0, 2, 3)
    return np.ascontiguousarray(both.astype(np.float32))


def small_tables():
    eye, one = np.eye(P), np.ones((P, P))
    upper = np.triu(np.ones((P, P)), 1)
    row = np.broadcast_to(np.arange(P), (P, P))
    tok = np.arange(P)[:, None] + P * np.arange(32)[None, :]
    return np.ascontiguousarray(np.concatenate([eye, one, upper, row, tok], 1).astype(np.float32))


class Columns:

    count = 0

    def __init__(self, nc, start, end, dt=F32):
        self.nc, self.at, self.end, self.dt = nc, start, end, dt

    def take(self, width, pattern=None, rows=P, **sizes):
        assert self.at + width <= self.end, (self.at, width, self.end)
        Columns.count += 1
        with ExitStack() as place:
            if self.at:
                place.enter_context(self.nc.sbuf_tensor(f"before{Columns.count}", [P, self.at], F32))
            tensor = place.enter_context(self.nc.sbuf_tensor(f"buffer{Columns.count}", [P, width], self.dt))
        self.at += -(-width // 16) * 16
        ap = tensor[0:rows, :]
        return ap.rearrange(pattern, **sizes) if pattern else ap


def build(nc, I, O):
    ctx = ExitStack()
    with ctx:
        SB_COLS = 53000
        PS = ctx.enter_context(nc.psum_tensor("PS", [P, 8 * 512], F32))

        def bank(b, width=512, rows=P, at=0):
            return PS[0:rows, 512 * b + at:512 * b + at + width]

        def dram(name, shape, dt=F32):
            return nc.dram_tensor(name, shape, dt, kind="Internal").ap()

        mod_d = dram("mod_rows", [2, 6 * D])
        spec_d = dram("filter_spectra", [2, NCLS + CCLS, 2, P, HW])
        h2_d = dram("moe_inputs", [T, D])
        slot_y_d = dram("slot_outputs", [MAX_BLOCKS * P, D])

        sems = {}

        def sem(name):
            if name not in sems:
                sems[name] = ctx.enter_context(nc.semaphore(name))
            return sems[name]

        keep = Columns(nc, 0, 4096)
        tables = keep.take(4 * P + 32)
        ident, ones, upper, row128 = (tables[:, P * i:P * (i + 1)] for i in range(4))
        token_no = tables[:, 4 * P:4 * P + 32]
        ntime = keep.take(NTILE)
        N_COLS = 36 + 12 + 8 + 8 + 16 + 16
        cols = keep.take(N_COLS)
        taps = cols[:, 0:36].rearrange("p (f w) -> p f w", w=3)
        tap_bias = cols[:, 36:48]
        skip_col = cols[:, 48:56].rearrange("p (o c) -> p o c", o=2)
        out_gain = cols[:, 56:64]
        bmod_col = cols[:, 64:80].rearrange("p (s k) -> p s k", s=2)
        cond = cols[:, 80:96].rearrange("p (c k) -> p c k", c=2)
        cond_silu = keep.take(16, "p (k c) -> p k c", c=2)
        mod_col = keep.take(32, "p (c s k) -> p c s k", c=2, s=2)
        qk_gain = keep.take(640)
        route_bias = keep.take(ROUTE_W)
        hid_cols = keep.take(P)
        w1_sb = keep.take(HID)
        col_v = keep.take(8)
        col_t = keep.take(8)
        col_r = keep.take(16, "p (o i) -> p o i", o=2)
        col_s = keep.take(8)
        tap_s = keep.take(12 * 8, "p (f l w) -> p f l w", l=2, w=4)
        bias_ring = keep.take(CHUNK)
        mod_ring = keep.take(2 * CHUNK, "p (r n) -> p r n", r=2)
        stat = keep.take(3 * 144, "p (a n) -> p a n", a=3)
        logits = keep.take(NTILE * ROUTE_W, "p (t e) -> p t e", t=NTILE)
        slot_token = keep.take(MAX_BLOCKS).bitcast(I32)
        control = keep.take(64, rows=1).bitcast(I32)
        slot_of = keep.take(2 * NTILE).bitcast(I32)
        mix_w = keep.take(2 * NTILE, "p (c t) -> p c t", c=2)
        bn = keep.take(48)
        token_col = keep.take(2).bitcast(I32)

        MATS0, WR0, HB0, TOP0 = 4096, 12032, 18176, 27392
        low = Columns(nc, MATS0, TOP0)
        mats = low.take(N_MATS * P, "p (m q) -> p m q", q=P)
        wring = low.take(2 * KT * CHUNK, "p (r k n) -> p r k n", r=2, k=KT)
        hbuf = low.take(2 * NTILE * HW)
        xT = hbuf.rearrange("p (k t) -> p k t", k=KT)
        hbuf = hbuf.rearrange("p (d j c) -> p d j c", d=2, j=NTILE)

        top = Columns(nc, TOP0, SB_COLS)
        h2T = top.take(T)
        w3 = top.take(4 * HW)
        decay = top.take(4 * HW)
        AF_f = top.take(16 * HW, "p (i c) -> p i c", i=16)
        TT_f = top.take(10 * HW, "p (i c) -> p i c", i=10)
        win = top.take(4 * HW, "p (r c) -> p r c", r=4)
        sq = top.take(2 * HW, "p (r c) -> p r c", r=2)
        spec_out = top.take(3 * HW, "p (r c) -> p r c", r=3)
        feats = AF_f[0:POS, 0:3, :].rearrange("p i c -> p (i c)")[:, 0:T]
        h1T = AF_f[0:HID, 3:6, :].rearrange("p i c -> p (i c)")[:, 0:T]
        arg = AF_f[0:HID, 6:9, :].rearrange("p i c -> p (i c)")[:, 0:T]
        turns = AF_f[0:HID, 9:12, :].rearrange("p i c -> p (i c)")[:, 0:T]
        norms = AF_f[:, 12:14, :]

        top = Columns(nc, TOP0, SB_COLS)
        qkv = top.take(NTILE * QKVW, "p (t n) -> p t n", t=NTILE)
        U0 = top.at
        U = [top.take(NTILE * HW, "p (t n) -> p t n", t=NTILE) for _ in range(3)]
        TAIL0 = top.at
        uc = top.take(2 * T, "p (r t) -> p r t", r=2)
        rope = Columns(nc, 50560, SB_COLS)
        rot = rope.take(NLAT * 2 * HD, "p (t s d) -> p t s d", t=NLAT, s=2)
        qk_work = rope.take(640)
        swap = rope.take(640)

        low = Columns(nc, WR0, TOP0)
        AF_h = low.take(16 * HW, "p (i c) -> p i c", i=16)
        TT_h = low.take(10 * HW, "p (i c) -> p i c", i=10)
        prod = low.take(4 * HW, "p (i c) -> p i c", i=4)
        tail = Columns(nc, TAIL0, SB_COLS)
        gbuf = tail.take(4 * HW, "p (r i c) -> p r i c", r=2, i=2)
        wbuf = tail.take(4 * HW, "p (r i c) -> p r i c", r=2, i=2)

        low = Columns(nc, MATS0, TOP0, F32R)
        qT = low.take(HEADS * T, "p (h t) -> p h t", h=HEADS)
        kT = low.take(4 * 10 * P, "p (s v t) -> p s v t", s=2, v=KV)
        q_split = low.take(2 * 2 * HEADS * HD, "p (r h s d) -> p r h s d", r=2, h=HEADS, s=2)
        k_split = low.take(2 * 2 * KV * 2 * HD, "p (r s v c d) -> p r s v c d", r=2, s=2, v=KV, c=2)
        low = Columns(nc, low.at, TOP0)
        probs = low.take(2 * NTILE * P, "p (r n) -> p r n", r=2)
        probsT = low.take(2 * NTILE * P, "p (r t n) -> p r t n", r=2, t=NTILE)
        mix_sq = low.take(2 * HW, "p (s c) -> p s c", s=2)
        tail = Columns(nc, TAIL0, SB_COLS)
        attn = tail.take(NTILE * HW, "p (t n) -> p t n", t=NTILE)
        gates = Columns(nc, U0 + NTILE * HW, TAIL0)
        cache_k = gates.take(P)
        cache_v = gates.take(P)
        nmax = gates.take(72)
        psums = gates.take(72)
        precip = gates.take(72)
        route_w = gates.take(KT * ROUTE_W, "p (k n) -> p k n", k=KT)
        w_out = gates.take(KT * D, "p (k n) -> p k n", k=KT)
        zeros = w_out[:, 0, :]

        x1 = Columns(nc, MATS0, TOP0).take(NTILE * D, "p (t n) -> p t n", t=NTILE)
        KT0, SPLIT0 = MATS0 + HEADS * T, MATS0 + HEADS * T + 4 * 10 * P
        low = Columns(nc, KT0, SPLIT0)
        sh2, sc2 = ([low.take(D) for _ in range(2)] for _ in range(2))
        ln1_b = low.take(D)
        low = Columns(nc, SPLIT0, TOP0)
        g1 = [low.take(D) for _ in range(2)]
        ln1_g = low.take(D)
        g2 = [low.take(D) for _ in range(2)]
        resid = low.take(D)
        xnorm = low.take(D)
        h2Tt = low.take(KT * P, "p (k n) -> p k n", k=KT)
        low = Columns(nc, TOP0, U0)
        mixT = low.take(2 * KT * P, "p (r k n) -> p r k n", r=2, k=KT)
        xres = low.take(2 * D, "p (r n) -> p r n", r=2)
        h2buf = low.take(2 * D, "p (r n) -> p r n", r=2)

        rt = Columns(nc, KT0, SPLIT0 + 3 * D)
        r_eq = rt.take(NTILE * NGRP, "p (t g) -> p t g", t=NTILE)
        r_g = rt.take(NTILE * NGRP, "p (t g) -> p t g", t=NTILE)
        r_exp = rt.take(NTILE * NGRP, "p (t g) -> p t g", t=NTILE)
        r_max = rt.take(NTILE)
        r_min = rt.take(NTILE)
        r_pg = rt.take(NTILE)
        r_v = rt.take(2 * NTILE, "p (c t) -> p c t", c=2)
        r_d = rt.take(NTILE)
        r_prod = rt.take(NTILE * NEXP, "p (t g e) -> p t g e", t=NTILE, g=NGRP)
        r_sel = rt.take(NTILE * EPG, "p (t e) -> p t e", t=NTILE)
        r_cand = rt.take(NTILE * EPG, "p (t e) -> p t e", t=NTILE)
        r_pick = rt.take(2 * NTILE * EPG, "p (c t e) -> p c t e", c=2, t=NTILE)
        r_mask = rt.take(2 * NTILE * NEXP, "p (c t n) -> p c t n", c=2, t=NTILE)
        r_all = rt.take(NTILE * NEXP, "p (t n) -> p t n", t=NTILE)
        r_before = rt.take((NTILE + 1) * NEXP, "p (t n) -> p t n", t=NTILE + 1)
        r_count = rt.take(NEXP)
        r_blocks = rt.take(NEXP)
        r_scan = rt.take(2 * NEXP, "p (r n) -> p r n", r=2)
        r_base = rt.take(NEXP)
        r_slot = rt.take(NTILE * NEXP, "p (t n) -> p t n", t=NTILE)
        r_pos = rt.take(2 * NTILE)
        r_int = rt.take(4 * NTILE).bitcast(I32)
        r_rowblk = rt.take(4 * NTILE, "p (a n) -> p a n", a=2)
        r_hot = rt.take(2 * NTILE * P, "p (i n) -> p i n", i=2 * NTILE)
        r_tok = rt.take(2 * NTILE * MAX_BLOCKS, "p (i n) -> p i n", i=2 * NTILE)
        r_cmp = r_hot.rearrange("p i n -> p (i n)")[:, 0:MAX_BLOCKS * NEXP].rearrange("p (b n) -> p b n", b=MAX_BLOCKS)
        r_eid = rt.take(64)

        ex = Columns(nc, U0, TAIL0)
        w_gu = ex.take(2 * 2 * KT * FF, "p (r g k f) -> p r g k f", r=2, g=2, k=KT)
        w_dn = ex.take(2 * 2 * D, "p (r s n) -> p r s n", r=2, s=2)
        ex = Columns(nc, TOP0, U0)
        ybuf = ex.take(2 * D, "p (r n) -> p r n", r=2)
        hT = ex.take(2 * 2 * P, "p (r s n) -> p r s n", r=2, s=2)
        gate_act = ex.take(2 * 2 * P, "p (r s n) -> p r s n", r=2, s=2)
        ln2_g, ln2_b = (ex.take(D) for _ in range(2))
        ex = Columns(nc, TAIL0, SB_COLS)
        xg = ex.take(2 * D, "p (r n) -> p r n", r=2)
        xgT = ex.take(2 * KT * P, "p (r k n) -> p r k n", r=2, k=KT)

        YG, YN = 4, 3
        fin = Columns(nc, U0, TAIL0)
        yg = fin.take(YG * 2 * D, "p (r c n) -> p r c n", r=YG, c=2)
        acc = fin.take(YN * D, "p (r n) -> p r n", r=YN)
        ynorm = Columns(nc, TOP0, TOP0 + YN * D).take(YN * D, "p (r n) -> p r n", r=YN)

        rs = {"spec": [sem(f"spectrum_stored{r}") for r in range(3)]}

        def filter_items(o):
            return [(18 * o + 2 * j + d, j, d) for j in range(NTILE) for d in range(2)]

        CLS_ORDER = (0, 8, 4, 2, 6, 1, 3, 5, 7)
        PART_OF = {0: 1, 8: 1, 4: 1, 2: 2, 6: 2}

        def spectrum_items(o):
            out = []
            for part in range(2):
                for cls in [*range(NCLS, NCLS + CCLS), *CLS_ORDER]:
                    out.append((22 * o + len(out), part, cls))
            return out

        N_SPEC = 2 * 22
        SPEC_STORED = [16 * len(range(r, N_SPEC, 3)) for r in range(3)]

        def mat(cls, kind):
            if cls < NCLS:
                return mats[:, 6 * cls + kind, :]
            return mats[:, 6 * NCLS + 4 * (cls - NCLS) + {0: 0, 2: 1, 3: 2, 5: 3}[kind], :]

        ATT = [(h, t) for t in range(NTILE) for h in range(HEADS)]
        SQUARE_AT = {8 * t + 9: t for t in range(NLAT)}
        NORM_AT = {8 * t + 10: t for t in range(NLAT)}
        block = ctx.enter_context(nc.Block())

        @block.sync
        def _(sp):
            def load(dst, src, s, **kw):
                return sp.dma_start(dst, src, **kw).then_inc(sem(s), 16)

            load(cols, I["cols"], "small_loaded")
            load(tables, I["tables"], "small_loaded")
            load(ntime, I["ntime"], "small_loaded")
            load(feats, I["feats"], "small_loaded")
            load(w1_sb[0:POS, :], I["hy_f_w1"], "small_loaded")
            load(hid_cols[0:HID, 0:HID + 3], I["hid"], "small_loaded")
            load(w3[0:HID, :], I["hy_f_w3"], "small_loaded")
            load(decay, I["hy_decay"].partition_broadcast(P), "small_loaded")
            load(mats[:, 0:N_MATS // 2, :], I["mats"][:, 0:N_MATS // 2, :], "mats_loaded")
            load(mats[:, N_MATS // 2:, :], I["mats"][:, N_MATS // 2:, :], "mats_loaded")
            load(qk_gain, I["qk_gain"].partition_broadcast(P), "gains_loaded")
            load(rot, I["rot"], "rot_loaded")
            load(route_bias, I["route_bias"].partition_broadcast(P), "gains_loaded")
            w_mod = I["w_mod"].rearrange("(p k) n -> p k n", k=KT)
            for c in range(MOD_CHUNKS):
                if c >= 2:
                    sp.wait_ge(sem("mod_product"), c - 1)
                load(wring[:, c % 2, :, :], w_mod[:, :, CHUNK * c:CHUNK * (c + 1)], f"w_loaded{c % 2}")
            w_in = I["w_in"].rearrange("(p k) n -> p k n", k=KT)

            def load_w_in(c):
                load(wring[:, c % 2, :, :], w_in[:, :, CHUNK * c:CHUNK * (c + 1)], f"w_loaded{c % 2}")

            for c in range(2):
                sp.wait_ge(sem("mod_product"), MOD_CHUNKS - 1 + c)
                load_w_in(c)
            for r in range(2):
                sp.wait_ge(sem(f"mod_stored{r}"), 16 * (MOD_CHUNKS // 2))
            for c in range(2):
                for s in range(2):
                    load(mod_col[:, c, s, :], mod_d[c, D * s:D * (s + 1)].rearrange("(p k) -> p k", k=KT),
                         "mod_col_loaded")
            sp.wait_ge(sem("tiles_transformed"), 12)
            sp.wait_ge(sem("spectrum_product"), 22 + 13)
            load(xT[:, :, :], I["xT"].rearrange("(p k) t -> p k t", k=KT), "x_loaded")
            for c in range(2, IN_CHUNKS):
                if c < 4:
                    sp.wait_ge(sem("qkv_product"), NTILE * (c - 1))
                else:
                    sp.wait_ge(sem("feature_product"), 3 * (c - 3))
                load_w_in(c)
            for r in range(3):
                sp.wait_ge(rs["spec"][r], SPEC_STORED[r])
            sp.wait_ge(sem("tokens_product"), 3 * FEATS)
            for q in range(2 * (NCLS + CCLS)):
                if q >= 2:
                    sp.wait_ge(sem("w_ready"), q - 1)
                o, idx = divmod(q, NCLS + CCLS)
                cls = CLS_ORDER[idx] if idx < NCLS else idx
                load(gbuf[:, q % 2, :, :], spec_d[o, cls].rearrange("i p c -> p i c"), f"g_loaded{q % 2}")
            sp.wait_ge(sem("hyena_done"), 1)
            load(cache_k, I["cache_k"], "cache_loaded")
            load(cache_v, I["cache_v"], "cache_loaded")
            load(O["new_k"], qkv[:, NLAT, HEADS * HD:(HEADS + KV) * HD], "out_stored")
            load(O["new_v"], qkv[:, NLAT, (HEADS + KV) * HD:QKVW], "out_stored")
            load(route_w, I["route_w"].rearrange("(k p) n -> p k n", p=P), "route_w_loaded")
            sp.wait_ge(sem("zeros_ready"), 1)
            for b in range(0, MAX_BLOCKS, 10):
                load(slot_y_d[P * b:P * (b + 10), :].rearrange("(b p) n -> p b n", p=P),
                     zeros.unsqueeze(1).broadcast_to([P, 10, D]), "slots_zeroed")

            def load_mod(dst, c, s, name):
                load(dst, mod_d[c, D * s:D * (s + 1)].partition_broadcast(P), name)

            sp.wait_ge(sem("qk_transposed"), 10)
            for c in range(2):
                load_mod(g1[c], c, 2, "g1_loaded")
            load(ln1_g, I["ln1_g"].partition_broadcast(P), "ln1_loaded")
            sp.wait_ge(sem("slots_zeroed"), 16 * 5)
            load(w_out, I["w_out"].rearrange("(k p) n -> p k n", p=P), "w_out_loaded")
            sp.wait_ge(sem("out_stored"), 32)
            sp.wait_ge(sem("scores_ready"), len(ATT))
            load(ln1_b, I["ln1_b"].partition_broadcast(P), "ln1_loaded")
            for c in range(2):
                load_mod(sc2[c], c, 4, "h2_rows_loaded")
                load_mod(sh2[c], c, 3, "h2_rows_loaded")
            sp.wait_ge(sem("attn_out"), len(ATT))
            x_tok = I["x_tok"].rearrange("(t p) n -> t p n", p=P)
            for t in range(2):
                load(xres[:, t, :], x_tok[t], f"xres_loaded{t % 2}")
            for c in range(2):
                load_mod(g2[c], c, 5, "g2_loaded")
            for t in range(NTILE):
                if t >= 2:
                    sp.wait_ge(sem("resid_ready"), t - 1)
                    load(xres[:, t % 2, :], x_tok[t], f"xres_loaded{t % 2}")
                sp.wait_ge(sem("h2_ready"), t + 1)
                load(h2_d[P * t:P * (t + 1), :], h2buf[:, t % 2, :], f"h2_stored{t % 2}")
            sp.wait_ge(sem("control_ready"), 1)
            pairs = sp.value_load(control[0:1, 60:61], min_val=1, max_val=MAX_BLOCKS // 2)
            with sp.Fori(0, pairs) as i:
                for u in range(2):
                    e = sp.value_load(control[0:1, bass.ds(2 * i + u, 1)], min_val=0, max_val=NEXP - 1)
                    sp.wait_ge(sem("gate_up_product"), 2 * i + u + 1)
                    for g, name in enumerate(("exp_w_gate", "exp_w_up")):
                        load(w_gu[:, u, g, :, :].rearrange("p k f -> p (k f)"),
                             I[name][bass.ds(e, 1), :, :].rearrange("e (p k) f -> p (e k f)", k=KT), f"we_loaded{u}")
                for u in range(2):
                    e = sp.value_load(control[0:1, bass.ds(2 * i + u, 1)], min_val=0, max_val=NEXP - 1)
                    sp.wait_ge(sem("block_done"), 2 * i + u + 1)
                    load(w_dn[:, u, :, :].rearrange("p s n -> p (s n)"),
                         I["exp_w_down"][bass.ds(e, 1), :, :].rearrange("e (p s) n -> p (e s n)", s=2), f"wd_loaded{u}")
            for t in range(NTILE):
                sp.wait_ge(sem("y_ready"), t + 1)
                out = O["lat"][P * t:P * (t + 1), :] if t < NLAT else O["ctx"]
                load(out, ynorm[:, t % YN, :], f"y_stored{t % YN}")
            for r in range(YN):
                sp.wait_ge(sem(f"y_stored{r}"), 16 * len(range(r, NTILE, YN)))

        @block.gpsimd
        def _(pool):
            scales = 0
            pool.memset(h2T[HID:P, :], 0.0).then_inc(sem("pads_zero"), 1)
            pool.memset(w3[HID:P, :], 0.0).then_inc(sem("pads_zero"), 1)
            pool.wait_ge(sem("pads_zero"), 2)
            for c in range(MOD_CHUNKS):
                at = CHUNK * c
                pool.dma_start(bias_ring[0:2, :], I["b_mod"][at:at + CHUNK].partition_broadcast(2)).then_inc(sem("bias_loaded"), 16)
                pool.wait_ge(sem("bias_loaded"), 16 * (c + 1))
                pool.wait_ge(sem("mod_copied"), c + 1)
                piece = mod_ring[0:2, c % 2, :]
                pool.tensor_tensor(piece, piece, bias_ring[0:2, :], ALU.add).then_inc(sem("mod_biased"), 1)
                pool.wait_ge(sem("mod_biased"), c + 1)
                for s in (1, 4):
                    a, b = max(D * s, at) - at, min(D * (s + 1), at + CHUNK) - at
                    if a < b:
                        scales += 1
                        pool.tensor_scalar(piece[:, a:b], piece[:, a:b], 1.0, None, ALU.add).then_inc(sem("scale_raised"), 1)
                        pool.wait_ge(sem("scale_raised"), scales)
                pool.dma_start(mod_d[:, at:at + CHUNK], piece).then_inc(sem(f"mod_stored{c % 2}"), 16)
            pool.wait_ge(sem("hyena_done"), 1)
            pool.memset(zeros, 0.0).then_inc(sem("zeros_ready"), 1)
            pool.wait_ge(sem("ln1_loaded"), 32)
            pool.wait_ge(sem("h2_rows_loaded"), 64)
            n = 0
            for t in range(NTILE):
                c = int(t == NLAT)
                pool.wait_ge(sem("xnorm_ready"), t + 1)
                pool.tensor_tensor(x1[:, t, :], xnorm, ln1_g, ALU.mult).then_inc(sem("pool_step"), 1)
                pool.wait_ge(sem("pool_step"), n + 1)
                pool.tensor_tensor(x1[:, t, :], x1[:, t, :], ln1_b, ALU.add).then_inc(sem("pool_step"), 1)
                pool.wait_ge(sem("pool_step"), n + 2)
                if t >= 2:
                    pool.wait_ge(sem(f"h2_stored{t % 2}"), 16 * (t // 2))
                    pool.wait_ge(sem("h2T_product"), t - 1)
                pool.tensor_tensor(h2buf[:, t % 2, :], x1[:, t, :], sc2[c], ALU.mult).then_inc(sem("pool_step"), 1)
                pool.wait_ge(sem("pool_step"), n + 3)
                pool.tensor_tensor(h2buf[:, t % 2, :], h2buf[:, t % 2, :], sh2[c], ALU.add).then_inc(sem("h2_ready"), 1)
                n += 3
            pool.wait_ge(sem("h2_stored0"), 16 * 5)
            pool.wait_ge(sem("h2_stored1"), 16 * 4)
            pool.wait_ge(sem("route_done"), 1)
            pairs = pool.value_load(control[0:1, 60:61], min_val=1, max_val=MAX_BLOCKS // 2)
            with pool.Fori(0, pairs) as i:
                for u in range(2):
                    pool.wait_ge(sem("x_transposed"), 2 * i + u + 1)
                    pool.tensor_copy(token_col[:, u:u + 1], slot_token[:, bass.ds(2 * i + u, 1)]).then_inc(sem("token_col_ready"), 1)
                    pool.wait_ge(sem("token_col_ready"), 2 * i + u + 1)
                    pool.sem_inc(sem("gather_started"), 1)
                    pool.indirect_dma_start(
                        out=xg[:, u, :], out_offset=None, in_=h2_d[:, :],
                        in_offset=bass.IndirectOffsetOnAxis(ap=token_col[:, u:u + 1], axis=0)).then_inc(sem(f"xg_loaded{u}"), 16)
            for u in range(2):
                pool.wait_ge(sem(f"slot_y_stored{u}"), 16 * pairs + 16)
            pool.sem_inc(sem("gather_started"), 1)
            def gather_outputs(t):
                if t >= YG:
                    pool.wait_ge(sem("acc_ready"), t - YG + 1)
                for c in range(2):
                    at = NTILE * c + t
                    pool.indirect_dma_start(
                        out=yg[:, t % YG, c, :], out_offset=None, in_=slot_y_d[:, :],
                        in_offset=bass.IndirectOffsetOnAxis(ap=slot_of[:, at:at + 1], axis=0),
                    ).then_inc(sem(f"yg_loaded{t % YG}"), 16)

            for t in range(YG):
                gather_outputs(t)
            pool.wait_ge(sem("ln2_loaded"), 32)
            for t in range(NTILE):
                y = ynorm[:, t % YN, :]
                pool.wait_ge(sem("ynorm_ready"), t + 1)
                pool.tensor_tensor(y, y, ln2_g, ALU.mult).then_inc(sem("pool_step"), 1)
                n += 1
                pool.wait_ge(sem("pool_step"), n)
                pool.tensor_tensor(y, y, ln2_b, ALU.add).then_inc(sem("y_ready"), 1)
                if t + YG < NTILE:
                    gather_outputs(t + YG)

        @block.scalar
        def _(act):
            steps = [0]

            def own(ins):
                steps[0] += 1
                ins.then_inc(sem("act_step"), 1)
                act.wait_ge(sem("act_step"), steps[0])

            act.wait_ge(sem("small_loaded"), 16 * 8)
            act.activation(cond_silu[:, :, :], cond.rearrange("p c k -> p k c"), ACT.Silu).then_inc(sem("cond_ready"), 1)
            own(act.activation(decay, decay, ACT.Abs))
            for layer in range(2):
                act.wait_ge(sem("arg_ready"), layer + 1)
                dst = h1T if layer == 0 else h2T[0:HID, :]
                act.activation(dst, arg, ACT.Sin).then_inc(sem("sine_ready"), 1)

            def window(n, j, d, o):
                if n >= 4:
                    act.wait_ge(sem("taps_ready"), n - 3)
                act.activation(win[:, n % 4, :], decay[:, 2 * HW * d + HW * o:2 * HW * d + HW * (o + 1)], ACT.Exp,
                               scale=ntime[:, j:j + 1]).then_inc(sem("window_ready"), 1)

            for o in range(2):
                items = filter_items(o)
                for n, j, d in items[:2]:
                    window(n, j, d, o)
                for i, (n, j, d) in enumerate(items):
                    if i + 2 < len(items):
                        window(*items[i + 2], o)
                    act.wait_ge(sem("taps_ready"), n + 1)
                    if n >= 2:
                        act.wait_ge(sem("norm_product"), n - 1)
                    act.activation(sq[:, n % 2, :], hbuf[:, d, j, :], ACT.Square).then_inc(sem("square_ready"), 1)
                for c in range(8 * o, 8 * o + 8):
                    act.wait_ge(sem("mod_product"), c + 1)
                    if c >= 2:
                        act.wait_ge(sem(f"mod_stored{c % 2}"), 16 * (c // 2))
                    act.copy(mod_ring[0:2, c % 2, :], bank(3 + c % 2, CHUNK, rows=2)).then_inc(sem("mod_copied"), 1)
                for m, part, cls in spectrum_items(o):
                    act.wait_ge(sem("spectrum_product"), m + 1)
                    if m >= 3:
                        act.wait_ge(rs["spec"][m % 3], 16 * (m // 3))
                    act.copy(spec_out[:, m % 3, :], bank(m % 3)).then_inc(sem("spectrum_copied"), 1)
                    act.wait_ge(sem("spectrum_copied"), m + 1)
                    act.dma_start(spec_d[o, cls, part], spec_out[:, m % 3, :]).then_inc(rs["spec"][m % 3], 16)

            for m in range(QKV_CHUNKS * NTILE):
                c, t = divmod(m, NTILE)
                act.wait_ge(sem("qkv_product"), m + 1)
                act.copy(qkv[:, t, CHUNK * c:CHUNK * (c + 1)], bank(m % 4, CHUNK)).then_inc(sem("qkv_copied"), 1)
            def square_qk(t):
                if t:
                    act.wait_ge(sem("qk_ready"), t)
                act.activation(qk_work, qkv[:, t, 0:640], ACT.Square).then_inc(sem("qk_squared"), 1)

            act.wait_ge(sem("qkv_copied"), QKV_CHUNKS * NTILE)
            square_qk(0)
            for f in range(FEATS):
                if 1 <= f < NTILE:
                    square_qk(f)
                for i, tiles in enumerate(((0, 4), (4, 8), (8, 9))):
                    g = 3 * f + i
                    n = tiles[1] - tiles[0]
                    act.wait_ge(sem("tokens_product"), g + 1)
                    act.copy(U[f // 4][:, tiles[0]:tiles[1], P * (f % 4):P * (f % 4 + 1)],
                             bank(6 + g % 2, P * n).rearrange("p (t c) -> p t c", t=n)).then_inc(sem("tokens_copied"), 1)

            for o in range(2):
                for idx, k in enumerate(CLS_ORDER):
                    act.wait_ge(sem("inverse_product"), 11 * o + idx + 1)
                    b = 4 + 2 * ((NCLS * o + idx) % 2)
                    if k in (0, 8):
                        ins = act.copy(AF_h[:, k, :], bank(b))
                    else:
                        ins = act.copy(AF_h[:, k:k + 9:8, :], PS[:, 512 * b:512 * (b + 2)].rearrange("p (i c) -> p i c", i=2))
                    ins.then_inc(sem("inverse_copied"), 1)

            for s in range(10):
                b = 3 * (s % 2)
                act.wait_ge(sem("qk_transposed"), s + 1)
                tile = s if s < 8 else NLAT
                if s != 8:
                    act.copy(qT[:, :, P * tile:P * (tile + 1)],
                             PS[:, 512 * b:512 * (b + 2)].rearrange("p (h t) -> p h t", h=HEADS))
                act.copy(kT[:, :, :, P * s:P * (s + 1)],
                         bank(b + 2).rearrange("p (s v t) -> p s v t", s=2, v=KV)).then_inc(sem("qk_copied"), 1)

            def exponent(i):
                h, t = ATT[i]
                n = NTILE * P if t < NLAT else P
                act.wait_ge(sem("max_ready"), i + 1)
                if i >= 2:
                    act.wait_ge(sem("probs_transposed"), i - 1)
                act.activation(probs[:, i % 2, 0:n], PS[:, 0:n], ACT.Exp, bias=nmax[:, i:i + 1], scale=1.0,
                               accum_out=psums[:, i:i + 1]).then_inc(sem("exp_ready"), 1)

            def square_mixers(t):
                act.wait_ge(sem("attn_out"), HEADS * (t + 1))
                if t:
                    act.wait_ge(sem("mix_normed"), t)
                act.activation(mix_sq[:, 0, :], attn[:, t, :], ACT.Square).then_inc(sem("mix_squared"), 1)
                act.activation(mix_sq[:, 1, :], U[0][:, t, :], ACT.Square).then_inc(sem("mix_squared"), 1)

            exponent(0)
            for i in range(len(ATT)):
                if i + 1 < len(ATT):
                    exponent(i + 1)
                h, t = ATT[i]
                n = 4 if t < NLAT else 1
                act.wait_ge(sem("probs_transposed"), i + 1)
                if i >= 2:
                    act.wait_ge(sem("attn_product"), i - 1)
                act.copy(probsT[:, i % 2, 0:n, :], bank(3, P * n).rearrange("p (t n) -> p t n", t=n)).then_inc(sem("probsT_a"), 1)
                if i in SQUARE_AT:
                    square_mixers(SQUARE_AT[i])

            square_mixers(NLAT)

            def gain_half(t):
                act.wait_ge(sem("mix_transposed"), t + 1)
                if t >= 2:
                    act.wait_ge(sem("mix_product"), t - 1)
                for k in range(4):
                    ins = act.activation(mixT[:, t % 2, k, :], bank(0, P, at=P * k), ACT.Copy, scale=out_gain[:, k:k + 1])
                ins.then_inc(sem("mixT_a"), 1)

            gain_half(0)
            for step in range(NTILE + 2):
                if step + 1 < NTILE:
                    gain_half(step + 1)
                if step < 2:
                    continue
                t = step - 2
                act.wait_ge(sem("h2T_product"), t + 1)
                if t >= 1:
                    act.wait_ge(sem("logit_product"), t)
                act.copy(h2Tt[:, :, :], PS[:, 1024:2048].rearrange("p (k n) -> p k n", k=KT)).then_inc(sem("h2T_ready"), 1)
            act.wait_ge(sem("group_shifted"), 1)
            act.activation(r_exp[:, :, :], r_g[:, :, :], ACT.Exp).then_inc(sem("group_exp"), 1)
            act.wait_ge(sem("pair_shifted"), 1)
            act.activation(r_d, r_d, ACT.Exp).then_inc(sem("pair_exp"), 1)

            act.wait_ge(sem("route_done"), 1)
            pairs = act.value_load(control[0:1, 60:61], min_val=1, max_val=MAX_BLOCKS // 2)
            act.wait_ge(sem("h2_stored0"), 16 * 5)
            act.wait_ge(sem("h2_stored1"), 16 * 4)
            act.dma_start(ln2_g, I["ln2_g"].partition_broadcast(P)).then_inc(sem("ln2_loaded"), 16)
            act.dma_start(ln2_b, I["ln2_b"].partition_broadcast(P)).then_inc(sem("ln2_loaded"), 16)
            for u in range(2):
                act.sem_inc(sem(f"slot_y_stored{u}"), 16)
            act.sem_inc(sem("y_a"), 2)
            with act.Fori(0, pairs) as i:
                for u in range(2):
                    act.wait_ge(sem("gate_up_product"), 2 * i + u + 3)
                    act.activation(gate_act[:, u, :, :], bank(4 + u, 256).rearrange("p (s n) -> p s n", s=2),
                                   ACT.Silu).then_inc(sem("gate_ready"), 1)
                for u in range(2):
                    act.wait_ge(sem("block_done"), 2 * i + u + 3)
                    act.wait_ge(sem(f"slot_y_stored{u}"), 16 * i + 16)
                    act.copy(ybuf[:, u, 0:512], bank((6, 2)[u])).then_inc(sem("y_a"), 1)
                    act.wait_ge(sem("y_a"), 2 * i + u + 3)
                    act.wait_ge(sem("y_d"), 2 * i + u + 3)
                    act.dma_start(slot_y_d[bass.ds(256 * i + P * u, P), :], ybuf[:, u, :]).then_inc(sem(f"slot_y_stored{u}"), 16)

            def normalise(t):
                act.wait_ge(sem("stats_ready"), t + 1)
                if t >= YN:
                    act.wait_ge(sem(f"y_stored{t % YN}"), 16 * (t // YN))
                at = 16 * (t % YN)
                act.activation(ynorm[:, t % YN, :], acc[:, t % YN, :], ACT.Identity, bias=bn[:, at + 15:at + 16],
                               scale=bn[:, at + 14:at + 15]).then_inc(sem("ynorm_ready"), 1)

            for t in range(NTILE):
                act.wait_ge(sem(f"yg_loaded{t % YG}"), 32 * (t // YG + 1))
                if t >= YN:
                    act.wait_ge(sem("ynorm_ready"), t - YN + 1)
                act.activation(acc[:, t % YN, :], yg[:, t % YG, 0, :], ACT.Copy, scale=mix_w[:, 0, t:t + 1]).then_inc(
                    sem("first_weighted"), 1)
                if t:
                    normalise(t - 1)
            normalise(NTILE - 1)

        @block.tensor
        def _(pe):
            def mm(out, lhsT, rhs, start=True, stop=True):
                return nc.tensor.matmul(out, lhsT, rhs, start=start, stop=stop)

            def turn(out, in_):
                return nc.tensor.transpose(out, in_, ident)

            pe.wait_ge(sem("small_loaded"), 16 * 8)
            for layer in range(2):
                w = w1_sb[0:POS, :] if layer == 0 else hid_cols[0:HID, 0:HID]
                x = feats if layer == 0 else h1T
                if layer:
                    pe.wait_ge(sem("sine_ready"), 1)
                for c in range(3):
                    n = min(512, T - 512 * c)
                    last = mm(bank(c, n, rows=HID), w, x[:, 512 * c:512 * c + n])
                last.then_inc(sem("hidden_product"), 1)
            pe.wait_ge(sem("sine_ready"), 2)
            pe.wait_ge(sem("pads_zero"), 2)
            pe.wait_ge(sem("mats_loaded"), 32)

            def norm(n, j):
                pe.wait_ge(sem("square_ready"), n + 1)
                b, first, last = (5, n % 18 == 0, n % 18 == 15) if j < NLAT else (6, n % 18 == 16, n % 18 == 17)
                mm(bank(b), ones, sq[:, n % 2, :], first, last).then_inc(sem("norm_product"), 1)

            def modulation(c):
                pe.wait_ge(sem(f"w_loaded{c % 2}"), 16 * (c // 2 + 1))
                if c >= 2:
                    pe.wait_ge(sem("mod_copied"), c - 1)
                for k in range(KT):
                    last = mm(bank(3 + c % 2, CHUNK, rows=2), cond_silu[:, k, :], wring[:, c % 2, k, :], k == 0, k == KT - 1)
                last.then_inc(sem("mod_product"), 1)

            for o in range(2):
                items = filter_items(o)
                if o:
                    pe.wait_ge(sem("mod_copied"), 8)
                    pe.wait_ge(sem("skip_added"), 1)
                for i, (n, j, d) in enumerate(items):
                    if n >= 2:
                        pe.wait_ge(sem("taps_ready"), n - 1)
                    mm(bank(3 + n % 2), h2T[:, P * j:P * (j + 1)],
                       w3[:, 2 * HW * d + HW * o:2 * HW * d + HW * (o + 1)]).then_inc(sem("taps_product"), 1)
                    if i >= 2:
                        norm(*items[i - 2][:2])
                norm(*items[16][:2])
                norm(*items[17][:2])
                pe.wait_ge(sem("norms_ready"), o + 1)
                for i in range(8):
                    last = mm(bank(7, 1, at=i), norms[:, i // 4, P * (i % 4):P * (i % 4 + 1)], ident[:, 0:1])
                last.then_inc(sem("norm_col"), 1)
                pe.wait_ge(sem("taps_ready"), 18 * (o + 1))
                pe.wait_ge(sem("cond_ready"), 1)
                for c in range(8 * o, 8 * o + 4):
                    modulation(c)
                pe.wait_ge(sem("skip_scaled"), o + 1)
                for i in range(8):
                    last = mm(bank(7 if i < 4 else 6, P, rows=1, at=P * (i % 4)), col_s[:, i:i + 1], ident)
                last.then_inc(sem("skip_row"), 1)
                for c in range(8 * o + 4, 8 * o + 8):
                    modulation(c)
                for m, part, cls in spectrum_items(o):
                    pe.wait_ge(sem("tiles_transformed"), 3 * (2 * o + part) + (PART_OF.get(cls, 3) if cls < NCLS else 1))
                    if m >= 3:
                        pe.wait_ge(sem("spectrum_copied"), m - 2)
                    out = bank(m % 3)
                    if cls >= NCLS:
                        last = mm(out, mat(cls, 2 * part), hbuf[:, part, NLAT, :])
                    elif cls in (0, 8):
                        last = mm(out, mat(cls, 2 * part), AF_f[:, cls, :])
                    elif part == 0:
                        mm(out, mat(cls, 0), AF_f[:, cls, :], True, False)
                        last = mm(out, mat(cls, 1), AF_f[:, 8 + cls, :], False, True)
                    else:
                        mm(out, mat(cls, 2), AF_f[:, cls, :], True, False)
                        last = mm(out, mat(cls, 0), AF_f[:, 8 + cls, :], False, True)
                    last.then_inc(sem("spectrum_product"), 1)

            pe.wait_ge(sem("spectrum_copied"), N_SPEC)
            pe.wait_ge(sem("mod_copied"), MOD_CHUNKS)
            pe.wait_ge(sem("hT_ready"), 1)
            for m in range(QKV_CHUNKS * NTILE):
                c, t = divmod(m, NTILE)
                pe.wait_ge(sem(f"w_loaded{c % 2}"), 16 * (9 + c // 2))
                if m >= 4:
                    pe.wait_ge(sem("qkv_copied"), m - 3)
                for k in range(KT):
                    last = mm(bank(m % 4, CHUNK), xT[:, k, P * t:P * (t + 1)], wring[:, c % 2, k, :], k == 0, k == KT - 1)
                last.then_inc(sem("qkv_product"), 1)
            pe.wait_ge(sem("qkv_copied"), QKV_CHUNKS * NTILE)

            def to_tokens(f):
                pe.wait_ge(sem("conv_ready"), f + 1)
                for i, tiles in enumerate((range(0, 4), range(4, 8), range(8, 9))):
                    g = 3 * f + i
                    if g >= 2:
                        pe.wait_ge(sem("tokens_copied"), g - 1)
                    for a, t in enumerate(tiles):
                        last = turn(bank(6 + g % 2, P, at=P * a), uc[:, f % 2, P * t:P * (t + 1)])
                    last.then_inc(sem("tokens_product"), 1)

            for f in range(FEATS):
                c = QKV_CHUNKS + f // 3
                b = 3 * (f % 2)
                pe.wait_ge(sem(f"w_loaded{c % 2}"), 16 * (9 + c // 2))
                if f >= 2:
                    pe.wait_ge(sem("conv_ready"), f - 1)
                for part, (t0, t1) in enumerate(((0, 512), (512, 1024), (1024, T))):
                    for k in range(KT):
                        last = mm(bank(b + part, t1 - t0), wring[:, c % 2, k, P * (f % 3):P * (f % 3 + 1)], xT[:, k, t0:t1],
                                  k == 0, k == KT - 1)
                last.then_inc(sem("feature_product"), 1)
                if f:
                    to_tokens(f - 1)
            to_tokens(FEATS - 1)

            def forward(o, idx):
                q = 11 * o + idx
                b = 2 * (q % 2)
                k = CLS_ORDER[idx] if idx < NCLS else idx
                pe.wait_ge(sem("z_transformed"), 3 * o + (PART_OF.get(k, 3) if k < NCLS else 1))
                if q >= 2:
                    pe.wait_ge(sem("w_ready"), q - 1)
                if k in (0, 8) or k >= NCLS:
                    z = AF_h[:, k, :] if k < NCLS else U[0][:, NLAT, :]
                    mm(bank(b), mat(k, 0), z)
                    last = mm(bank(b + 1), mat(k, 2), z)
                else:
                    mm(bank(b), mat(k, 0), AF_h[:, k, :], True, False)
                    mm(bank(b), mat(k, 1), AF_h[:, 8 + k, :], False, True)
                    mm(bank(b + 1), mat(k, 2), AF_h[:, k, :], True, False)
                    last = mm(bank(b + 1), mat(k, 0), AF_h[:, 8 + k, :], False, True)
                last.then_inc(sem("z_product"), 1)

            def inverse(o, idx):
                q = 11 * o + idx
                k = CLS_ORDER[idx] if idx < NCLS else idx
                wr, wi = wbuf[:, q % 2, 0, :], wbuf[:, q % 2, 1, :]
                pe.wait_ge(sem("w_ready"), q + 1)
                if k < NCLS:
                    n = NCLS * o + idx
                    b = 4 + 2 * (n % 2)
                    if n >= 2:
                        pe.wait_ge(sem("inverse_copied"), n - 1)
                    mm(bank(b), mat(k, 3), wr, True, False)
                    last = mm(bank(b), mat(k, 5), wi, False, True)
                    if k not in (0, 8):
                        mm(bank(b + 1), mat(k, 4), wr, True, False)
                        last = mm(bank(b + 1), mat(k, 3), wi, False, True)
                else:
                    b = 6 - 2 * o
                    pe.wait_ge(sem("inverse_copied"), NCLS * o + 8)
                    mm(bank(b), mat(k, 3), wr, k == NCLS, False)
                    last = mm(bank(b), mat(k, 5), wi, False, k == NCLS + 1)
                last.then_inc(sem("inverse_product"), 1)

            pe.wait_ge(sem("tokens_copied"), 3 * FEATS)
            for o in range(2):
                forward(o, 0)
                for idx in range(NCLS + CCLS):
                    if idx + 1 < NCLS + CCLS:
                        forward(o, idx + 1)
                    inverse(o, idx)

            pe.wait_ge(sem("hyena_done"), 1)
            for s in range(10):
                b = 3 * (s % 2)
                pe.wait_ge(sem("split_ready"), s + 1)
                if s >= 2:
                    pe.wait_ge(sem("qk_copied"), s - 1)
                if s != 8:
                    for h in range(HEADS):
                        turn(bank(b + h // 4, P, at=P * (h % 4)),
                             q_split[:, s % 2, h, :, :].rearrange("p s d -> p (s d)").bitcast(F32))
                for a in range(4):
                    last = turn(bank(b + 2, P, at=P * a),
                                k_split[:, s % 2, a // 2, a % 2, :, :].rearrange("p c d -> p (c d)").bitcast(F32))
                last.then_inc(sem("qk_transposed"), 1)

            def scores(i):
                h, t = ATT[i]
                v = h // GQA
                pieces = ((0, 512), (512, 1024), (1024, 1152)) if t < NLAT else ((1152, 1280),)
                if i:
                    pe.wait_ge(sem("exp_ready"), i)
                for s in range(2):
                    for a, (k0, k1) in enumerate(pieces):
                        last = mm(bank(a, k1 - k0), qT[:, h, P * t:P * (t + 1)], kT[:, s, v, k0:k1], s == 0, s == 1)
                last.then_inc(sem("scores_ready"), 1)

            def turn_probs(i):
                n = NTILE if ATT[i][1] < NLAT else 1
                pe.wait_ge(sem("exp_ready"), i + 1)
                if i:
                    pe.wait_ge(sem("probsT_a"), i)
                    pe.wait_ge(sem("probsT_d"), i)
                for k in range(n):
                    last = turn(PS[:, 1536 + P * k:1536 + P * (k + 1)], probs[:, i % 2, P * k:P * (k + 1)])
                last.then_inc(sem("probs_transposed"), 1)

            def values(i):
                h, t = ATT[i]
                pe.wait_ge(sem("probsT_a"), i + 1)
                pe.wait_ge(sem("probsT_d"), i + 1)
                if i >= 2:
                    pe.wait_ge(sem("attn_out"), i - 1)
                tiles = [*range(NLAT), None] if t < NLAT else [NLAT]
                for a, k in enumerate(tiles):
                    v = cache_v if k is None else qkv[:, k, (HEADS + KV) * HD:QKVW]
                    last = mm(bank(6 + i % 2, P), probsT[:, i % 2, a, :], v, a == 0, a == len(tiles) - 1)
                last.then_inc(sem("attn_product"), 1)

            pe.wait_ge(sem("qk_copied"), 10)
            scores(0)
            for i in range(len(ATT)):
                if i + 1 < len(ATT):
                    scores(i + 1)
                turn_probs(i)
                if i:
                    values(i - 1)
            values(len(ATT) - 1)

            def turn_mix(t):
                pe.wait_ge(sem("mix_normed"), t + 1)
                if t:
                    pe.wait_ge(sem("mixT_a"), t)
                    pe.wait_ge(sem("mixT_d"), t)
                for k in range(KT):
                    src = (attn if k < 4 else U[0])[:, t, P * (k % 4):P * (k % 4 + 1)]
                    last = turn(bank(k // 4, P, at=P * (k % 4)), src)
                last.then_inc(sem("mix_transposed"), 1)

            def project_mix(t):
                pe.wait_ge(sem("mixT_a"), t + 1)
                pe.wait_ge(sem("mixT_d"), t + 1)
                if t >= 2:
                    pe.wait_ge(sem("resid_ready"), t - 1)
                for c in range(2):
                    for k in range(KT):
                        last = mm(bank(4 + 2 * (t % 2) + c), mixT[:, t % 2, k, :], w_out[:, k, 512 * c:512 * (c + 1)],
                                  k == 0, k == KT - 1)
                last.then_inc(sem("mix_product"), 1)

            def route(t):
                pe.wait_ge(sem("h2_ready"), t + 1)
                if t:
                    pe.wait_ge(sem("logits_ready"), t)
                for k in range(KT):
                    last = turn(bank(2 + k // 4, P, at=P * (k % 4)), h2buf[:, t % 2, P * k:P * (k + 1)])
                last.then_inc(sem("h2T_product"), 1)
                pe.wait_ge(sem("h2T_ready"), t + 1)
                for k in range(KT):
                    last = mm(bank(2, ROUTE_W), h2Tt[:, k, :], route_w[:, k, :], k == 0, k == KT - 1)
                last.then_inc(sem("logit_product"), 1)

            pe.wait_ge(sem("attn_out"), len(ATT))
            turn_mix(0)
            pe.wait_ge(sem("w_out_loaded"), 16)
            pe.wait_ge(sem("route_w_loaded"), 16)
            for t in range(NTILE + 2):
                if t + 1 < NTILE:
                    turn_mix(t + 1)
                if t < NTILE:
                    project_mix(t)
                if t >= 2:
                    route(t - 2)

            pe.wait_ge(sem("assigned"), 1)
            flat = "p t n -> p (t n)"
            mm(bank(0, NTILE * NEXP), upper, r_all[:, :, :].rearrange(flat), True, False)
            mm(bank(0, NTILE * NEXP), ones, r_before[:, 0:NTILE, :].rearrange(flat), False, True)
            mm(bank(1, NEXP), ones, r_before[:, NTILE, :]).then_inc(sem("rank_product"), 1)
            pe.sem_inc(sem("x_transposed"), 2)
            pe.sem_inc(sem("block_done"), 2)
            pe.sem_inc(sem("gate_up_product"), 2)
            pe.wait_ge(sem("hot_ready"), 1)
            for i in range(2 * NTILE):
                last = mm(bank(4, MAX_BLOCKS), r_hot[:, i, :], r_tok[:, i, :], i == 0, i == 2 * NTILE - 1)
            last.then_inc(sem("slot_product"), 1)

            pe.wait_ge(sem("route_done"), 1)
            pairs = pe.value_load(control[0:1, 60:61], min_val=1, max_val=MAX_BLOCKS // 2)
            with pe.Fori(0, pairs) as i:
                for u in range(2):
                    pe.wait_ge(sem(f"xg_loaded{u}"), 16 * i + 16)
                    pe.wait_ge(sem("y_a"), 2 * i + u + 1)
                    pe.wait_ge(sem("y_d"), 2 * i + u + 1)
                    for k in range(KT):
                        last = turn(bank(2 * u + k // 4, P, at=P * (k % 4)), xg[:, u, k:D:KT])
                    last.then_inc(sem("x_transposed"), 1)
                for u in range(2):
                    pe.wait_ge(sem("xT_ready"), 2 * i + u + 1)
                    pe.wait_ge(sem(f"we_loaded{u}"), 32 * i + 32)
                    for g in range(2):
                        for s in range(2):
                            for k in range(KT):
                                last = mm(bank(4 + u, P, at=256 * g + P * s), w_gu[:, u, g, k, s:FF:2], xgT[:, u, k, :],
                                          k == 0, k == KT - 1)
                    last.then_inc(sem("gate_up_product"), 1)
                for u in range(2):
                    pe.wait_ge(sem(f"wd_loaded{u}"), 16 * i + 16)
                    pe.wait_ge(sem("hidden_ready"), 2 * i + u + 1)
                    for c in range(2):
                        for s in range(2):
                            last = mm(bank((6, 2)[u] + c), hT[:, u, s, :], w_dn[:, u, s, 512 * c:512 * (c + 1)], s == 0, s == 1)
                    last.then_inc(sem("block_done"), 1)

        @block.vector
        def _(dve):
            steps = [0]

            def own(ins):
                steps[0] += 1
                ins.then_inc(sem("dve_step"), 1)
                dve.wait_ge(sem("dve_step"), steps[0])

            counts = {}

            def give(ins, name):
                counts[name] = counts.get(name, 0) + 1
                ins.then_inc(sem(name), 1)
                dve.wait_ge(sem(name), counts[name])

            def tt(out, a, b, op):
                return dve.tensor_tensor(out, a, b, op)

            def add(out, a, b):
                own(tt(out, a, b, ALU.add))

            def sub(out, a, b):
                own(tt(out, a, b, ALU.subtract))

            def scaled(out, a, s):
                own(dve.tensor_scalar(out, a, s, None, ALU.mult))

            def axpy(out, a, s, b, op=ALU.add):
                own(dve.scalar_tensor_tensor(out, a, s, b, ALU.mult, op))

            def rsqrt(out, v, tmp):
                own(dve.tensor_scalar(out.bitcast(I32), v.bitcast(I32), -0.5, RSQRT_SEED, ALU.mult, ALU.add))
                for scale in (1.0, 2.0, 16.0):
                    if out.shape[-1] == 1:
                        own(dve.scalar_tensor_tensor(tmp, out, out, v, ALU.mult, ALU.mult))
                    else:
                        own(tt(tmp, out, out, ALU.mult))
                        own(tt(tmp, tmp, v, ALU.mult))
                    own(dve.scalar_tensor_tensor(out, tmp, -3.0 * scale * scale, out, ALU.add, ALU.mult))
                own(dve.tensor_scalar(out, out, -1.0 / 8192, None, ALU.mult))

            def transform_tiles(A, W, X, name):
                own(tt(W[:, 0:4, :], X[:, 0:4, :], X[:, 4:8, :], ALU.add))
                own(tt(W[:, 4:8, :], X[:, 0:4, :], X[:, 4:8, :], ALU.subtract))
                w = [W[:, i, :] for i in range(10)]
                a = [A[:, i, :] for i in range(16)]
                x = [X[:, j, :] for j in range(8)]
                add(w[8], w[0], w[2])
                add(w[9], w[1], w[3])
                add(a[0], w[8], w[9])
                sub(a[8], w[8], w[9])
                sub(a[4], w[0], w[2])
                give(tt(a[12], w[3], w[1], ALU.subtract), name)
                sub(w[8], w[5], w[7])
                add(w[9], w[5], w[7])
                axpy(a[2], w[8], C2, w[4])
                axpy(a[6], w[8], -C2, w[4])
                axpy(a[10], w[9], -C2, w[6], ALU.subtract)
                give(dve.scalar_tensor_tensor(a[14], w[9], -C2, w[6], ALU.mult, ALU.add), name)
                own(tt(W[:, 0:3, :], X[:, 1:4, :], X[:, 7:4:-1, :], ALU.subtract))
                own(tt(W[:, 3:6, :], X[:, 1:4, :], X[:, 7:4:-1, :], ALU.add))
                axpy(w[6], w[1], C2, x[0])
                axpy(w[7], w[1], -C2, x[0])
                scaled(w[8], w[2], C3)
                axpy(w[8], w[0], C1, w[8])
                scaled(w[9], w[2], C1)
                axpy(w[9], w[0], C3, w[9], ALU.subtract)
                add(a[1], w[6], w[8])
                sub(a[7], w[6], w[8])
                add(a[3], w[7], w[9])
                sub(a[5], w[7], w[9])
                axpy(w[6], w[4], C2, x[4])
                axpy(w[7], w[4], C2, x[4], ALU.subtract)
                scaled(w[8], w[5], C1)
                axpy(w[8], w[3], C3, w[8])
                scaled(w[9], w[5], C3)
                axpy(w[9], w[3], C1, w[9], ALU.subtract)
                axpy(a[9], w[8], -1.0, w[6], ALU.subtract)
                sub(a[15], w[6], w[8])
                axpy(a[11], w[9], -1.0, w[7], ALU.subtract)
                give(tt(a[13], w[7], w[9], ALU.subtract), name)

            def combine_tiles(A, W, gate, z):
                w = [W[:, i, :] for i in range(10)]
                a = [A[:, i, :] for i in range(16)]
                add(w[0], a[0], a[8])
                sub(w[1], a[0], a[8])
                add(a[0], w[0], a[4])
                sub(a[8], w[0], a[4])
                sub(w[0], w[1], a[12])
                add(a[4], w[1], a[12])
                add(w[1], a[2], a[6])
                sub(w[2], a[14], a[10])
                sub(w[3], a[2], a[6])
                add(a[2], a[10], a[14])
                sub(a[6], w[3], a[2])
                add(a[10], w[3], a[2])
                add(a[2], a[0], w[1])
                sub(a[14], a[0], w[1])
                add(a[0], a[8], w[2])
                sub(a[12], a[8], w[2])
                axpy(a[8], a[6], C2, w[0])
                axpy(w[1], a[6], -C2, w[0])
                axpy(w[2], a[10], -C2, a[4])
                axpy(w[3], a[10], C2, a[4])
                add(w[4], a[1], a[7])
                sub(w[5], a[1], a[7])
                add(w[6], a[3], a[5])
                sub(w[7], a[3], a[5])
                add(a[1], a[9], a[15])
                sub(a[7], a[9], a[15])
                add(a[3], a[11], a[13])
                sub(a[5], a[11], a[13])
                add(w[8], w[4], w[6])
                sub(w[9], w[4], w[6])
                scaled(w[4], w[5], C1)
                axpy(w[4], w[7], C3, w[4])
                scaled(w[6], w[5], C3)
                axpy(w[6], w[7], -C1, w[6])
                scaled(a[9], a[1], C3)
                axpy(a[9], a[3], C1, a[9])
                scaled(a[11], a[1], C1)
                axpy(a[11], a[3], -C3, a[11])
                add(a[13], a[7], a[5])
                sub(a[15], a[7], a[5])
                add(a[1], a[2], w[8])
                sub(a[3], a[14], a[15])
                sub(w[0], w[9], a[13])
                add(w[5], w[9], a[13])
                axpy(a[5], w[0], C2, a[0])
                axpy(a[7], w[5], -C2, a[12])
                sub(w[7], w[4], a[9])
                add(w[9], w[4], a[9])
                add(a[4], a[8], w[7])
                sub(a[6], w[3], w[9])
                sub(w[7], w[6], a[11])
                add(w[9], w[6], a[11])
                add(a[9], w[2], w[7])
                sub(a[10], w[1], w[9])
                for j, y in enumerate((a[1], a[4], a[5], a[9], a[3], a[10], a[7], a[6])):
                    own(tt(z[:, j, :], gate[:, j, :], y, ALU.mult))

            dve.wait_ge(sem("small_loaded"), 16 * 8)
            freq = hid_cols[0:HID, HID + 2:HID + 3]
            for layer in range(2):
                own(tt(hid_cols[0:HID, HID + 3 + layer:HID + 4 + layer], hid_cols[0:HID, HID + layer:HID + layer + 1], freq, ALU.mult))
            for layer in range(2):
                dve.wait_ge(sem("hidden_product"), layer + 1)
                own(dve.tensor_scalar(arg, PS[0:HID, 0:T], freq, hid_cols[0:HID, HID + 3 + layer:HID + 4 + layer], ALU.mult, ALU.add))
                own(dve.tensor_scalar(turns, arg, float(1 / (2 * np.pi)), ROUND_MAGIC, ALU.mult, ALU.add))
                own(dve.tensor_scalar(turns, turns, -ROUND_MAGIC, None, ALU.add))
                axpy(arg, turns, -TWO_PI_HI, arg)
                axpy(arg, turns, -TWO_PI_LO, arg)
                give(dve.tensor_scalar(arg, arg, PI_BELOW, -PI_BELOW, ALU.min, ALU.max), "arg_ready")

            for o in range(2):
                if o:
                    dve.wait_ge(sem("square_ready"), 18)
                    dve.wait_ge(sem("spectrum_product"), 22)
                for n, j, d in filter_items(o):
                    dve.wait_ge(sem("taps_product"), n + 1)
                    dve.wait_ge(sem("window_ready"), n + 1)
                    taps_out = tt(hbuf[:, d, j, :], bank(3 + n % 2), win[:, n % 4, :], ALU.mult)
                    if d == 1 and j in (0, NLAT):
                        own(taps_out)
                        taps_out = dve.memset(hbuf[0:1, d, j, :], 0.0)
                    give(taps_out, "taps_ready")
                dve.wait_ge(sem("norm_product"), 18 * (o + 1))
                own(dve.tensor_copy(norms[:, 0, :], bank(5)))
                give(dve.tensor_copy(norms[:, 1, :], bank(6)), "norms_ready")
                dve.wait_ge(sem("norm_col"), o + 1)
                own(dve.tensor_scalar(col_v, bank(7, 8), EPS, None, ALU.add))
                rsqrt(col_r[:, o, :], col_v, col_t)
                own(tt(col_s, col_v, col_r[:, o, :], ALU.mult))
                own(tt(col_s[:, 0:4], col_s[:, 0:4], skip_col[:, o, :], ALU.mult))
                give(tt(col_s[:, 4:8], col_s[:, 4:8], skip_col[:, o, :], ALU.mult), "skip_scaled")
                dve.wait_ge(sem("skip_row"), o + 1)
                own(tt(hbuf[0:1, 0, 0, :], hbuf[0:1, 0, 0, :], bank(7, rows=1), ALU.add))
                give(tt(hbuf[0:1, 0, NLAT, :], hbuf[0:1, 0, NLAT, :], bank(6, rows=1), ALU.add), "skip_added")
                dve.wait_ge(sem("square_ready"), 18 * (o + 1))
                add(hbuf[:, 0, :, :], hbuf[:, 0, :, :], hbuf[:, 1, :, :])
                axpy(hbuf[:, 1, :, :], hbuf[:, 1, :, :], -2.0, hbuf[:, 0, :, :])
                transform_tiles(AF_f, TT_f, hbuf[:, 0, 0:NLAT, :], "tiles_transformed")
                dve.wait_ge(sem("spectrum_product"), 22 * o + 11)
                transform_tiles(AF_f, TT_f, hbuf[:, 1, 0:NLAT, :], "tiles_transformed")

            dve.wait_ge(sem("mod_col_loaded"), 64)
            dve.wait_ge(sem("x_loaded"), 16)
            for k in range(KT):
                for c, (t0, t1) in enumerate(((0, LAT), (LAT, T))):
                    ins = dve.tensor_scalar(xT[:, k, t0:t1], xT[:, k, t0:t1], mod_col[:, c, 1, k:k + 1], mod_col[:, c, 0, k:k + 1],
                                            ALU.mult, ALU.add)
                    own(ins) if (k, c) != (KT - 1, 1) else give(ins, "hT_ready")

            for lc in range(2):
                own(dve.tensor_copy(tap_s[:, 0:4, lc, 0:3], taps[:, 0:4, :]))
                own(dve.tensor_copy(tap_s[:, 0:4, lc, 3], tap_bias[:, 0:4]))
                for o in range(2):
                    f = slice(4 * o + 4, 4 * o + 8)
                    r = col_r[:, o, 4 * lc:4 * lc + 4]
                    own(tt(tap_s[:, f, lc, 0:3], taps[:, f, :], r.unsqueeze(2).broadcast_to([P, 4, 3]), ALU.mult))
                    own(tt(tap_s[:, f, lc, 3], tap_bias[:, f], r, ALU.mult))
            for r in range(3):
                dve.wait_ge(rs["spec"][r], SPEC_STORED[r])
            heads = "p (h d) -> p h d"
            quarters = "p (h a s f) -> p h a s f"

            def norm_and_rotate(t):
                x = qkv[:, t, 0:640]
                xh = x.rearrange(heads, h=10)
                v, r, tmp = (stat[:, i, 0:10] for i in range(3))
                dve.wait_ge(sem("qk_squared"), t + 1)
                own(dve.tensor_reduce(v, qk_work.rearrange(heads, h=10), AX.X, ALU.add))
                own(dve.tensor_scalar(v, v, 1.0 / HD, EPS, ALU.mult, ALU.add))
                rsqrt(r, v, tmp)
                own(tt(xh, xh, r.unsqueeze(2).broadcast_to([P, 10, HD]), ALU.mult))
                if t == NLAT:
                    return give(tt(x, x, qk_gain, ALU.mult), "qk_ready")
                own(tt(x, x, qk_gain, ALU.mult))
                own(tt(qk_work.rearrange(heads, h=10), xh, rot[:, t, 0, :].unsqueeze(1).broadcast_to([P, 10, HD]), ALU.mult))
                x5, s5 = (y.rearrange(quarters, h=10, a=2, s=2) for y in (x, swap))
                sin = rot[:, t, 1, :].rearrange("p (a s f) -> p a s f", a=2, s=2)
                for half in range(2):
                    own(tt(s5[:, :, :, half, :], x5[:, :, :, 1 - half, :],
                           sin[:, :, half, :].unsqueeze(1).broadcast_to([P, 10, 2, 16]), ALU.mult))
                give(tt(x, qk_work, swap, ALU.add), "qk_ready")

            dve.wait_ge(sem("rot_loaded"), 16)
            dve.wait_ge(sem("gains_loaded"), 32)
            scaled(qk_gain[:, 0:HEADS * HD], qk_gain[:, 0:HEADS * HD], HD ** -0.5)
            for f in range(FEATS):
                ps0 = 1536 * (f % 2)
                dve.wait_ge(sem("feature_product"), f + 1)
                if f >= 2:
                    dve.wait_ge(sem("tokens_product"), 3 * (f - 1))
                out = uc[:, f % 2, :]
                for lc, (t0, t1) in enumerate(((0, LAT), (LAT, T))):
                    w = [tap_s[:, f, lc, i:i + 1] for i in range(4)]
                    own(dve.tensor_scalar(out[:, t0:t1], PS[:, ps0 + t0:ps0 + t1], w[1], w[3], ALU.mult, ALU.add))
                    axpy(out[:, t0 + 1:t1], PS[:, ps0 + t0:ps0 + t1 - 1], w[0], out[:, t0 + 1:t1])
                    ins = dve.scalar_tensor_tensor(out[:, t0:t1 - 1], PS[:, ps0 + t0 + 1:ps0 + t1], w[2], out[:, t0:t1 - 1],
                                                   ALU.mult, ALU.add)
                    own(ins) if lc == 0 else give(ins, "conv_ready")
                if f < NTILE:
                    norm_and_rotate(f)

            dve.wait_ge(sem("tokens_copied"), 3 * FEATS)
            for o in range(2):
                transform_tiles(AF_h, TT_h, U[0][:, 0:NLAT, :], "z_transformed")
                for idx in range(NCLS + CCLS):
                    q = 11 * o + idx
                    dve.wait_ge(sem("z_product"), q + 1)
                    dve.wait_ge(sem(f"g_loaded{q % 2}"), 16 * (q // 2 + 1))
                    b = 2 * (q % 2)
                    z = PS[:, 512 * b:512 * (b + 2)].rearrange("p (i c) -> p i c", i=2)
                    own(tt(prod[:, 0:2, :], z, gbuf[:, q % 2, :, :], ALU.mult))
                    own(tt(prod[:, 2:4, :], z, gbuf[:, q % 2, ::-1, :], ALU.mult))
                    if q >= 2:
                        dve.wait_ge(sem("inverse_product"), q - 1)
                    sub(wbuf[:, q % 2, 0, :], prod[:, 0, :], prod[:, 1, :])
                    give(tt(wbuf[:, q % 2, 1, :], prod[:, 2, :], prod[:, 3, :], ALU.add), "w_ready")
                dve.wait_ge(sem("inverse_product"), 11 * (o + 1))
                own(tt(U[0][:, NLAT, :], U[o + 1][:, NLAT, :], bank(6 - 2 * o), ALU.mult))
                dve.wait_ge(sem("inverse_copied"), NCLS * (o + 1))
                combine_tiles(AF_h, TT_h, U[o + 1], U[0])
            dve.sem_inc(sem("hyena_done"), 1)

            dve.wait_ge(sem("cache_loaded"), 32)
            for s in range(10):
                x = qkv[:, s if s < 8 else NLAT, 0:640]
                if s >= 2:
                    dve.wait_ge(sem("qk_transposed"), s - 1)
                r = s % 2
                if s != 8:
                    q = x[:, 0:HEADS * HD].rearrange(heads, h=HEADS)
                    own(dve.tensor_copy(q_split[:, r, :, 0, :], q))
                    own(tt(q_split[:, r, :, 1, :], q, q_split[:, r, :, 0, :].bitcast(F32), ALU.subtract))
                k = (cache_k if s == 8 else x[:, HEADS * HD:]).rearrange(heads, h=KV)
                kk = k.unsqueeze(2).broadcast_to([P, KV, 2, HD])
                own(dve.tensor_copy(k_split[:, r, 0, :, :, :], kk))
                give(tt(k_split[:, r, 1, :, :, :], kk, k_split[:, r, 0, :, :, :].bitcast(F32), ALU.subtract), "split_ready")

            def maximum(i):
                n = NTILE * P if ATT[i][1] < NLAT else P
                dve.wait_ge(sem("scores_ready"), i + 1)
                give(dve.tensor_reduce(nmax[:, i:i + 1], PS[:, 0:n], AX.X, ALU.max, negate=True), "max_ready")

            def weighted(i):
                h, t = ATT[i]
                dve.wait_ge(sem("attn_product"), i + 1)
                own(dve.reciprocal(precip[:, i:i + 1], psums[:, i:i + 1]))
                v = HD * (h // GQA)
                give(dve.tensor_scalar(attn[:, t, HD * h:HD * (h + 1)], bank(6 + i % 2, HD, at=v), precip[:, i:i + 1], None,
                                       ALU.mult), "attn_out")

            def norm_mixers(t):
                v, r, tmp = (stat[:, i, 0:16] for i in range(3))
                dve.wait_ge(sem("mix_squared"), 2 * t + 2)
                own(dve.tensor_reduce(v, mix_sq[:, :, :].rearrange("p s (g d) -> p (s g) d", g=8), AX.X, ALU.add))
                own(dve.tensor_scalar(v, v, 1.0 / HD, EPS, ALU.mult, ALU.add))
                rsqrt(r, v, tmp)
                for src in range(2):
                    x = (attn, U[0])[src][:, t, :].rearrange("p (g d) -> p g d", g=8)
                    ins = tt(x, x, r[:, 8 * src:8 * src + 8].unsqueeze(2).broadcast_to([P, 8, HD]), ALU.mult)
                    own(ins) if src == 0 else give(ins, "mix_normed")

            maximum(0)
            for i in range(len(ATT)):
                if i + 1 < len(ATT):
                    maximum(i + 1)
                dve.wait_ge(sem("probs_transposed"), i + 1)
                if i >= 2:
                    dve.wait_ge(sem("attn_product"), i - 1)
                if ATT[i][1] < NLAT:
                    give(dve.tensor_copy(probsT[:, i % 2, 4:9, :], PS[:, 2048:2688].rearrange("p (t n) -> p t n", t=5)), "probsT_d")
                else:
                    give(dve.tensor_copy(bn[:, 0:1], ones[:, 0:1]), "probsT_d")
                if i:
                    weighted(i - 1)
                if i in NORM_AT:
                    norm_mixers(NORM_AT[i])
            weighted(len(ATT) - 1)

            norm_mixers(NLAT)

            def gain_half(t):
                dve.wait_ge(sem("mix_transposed"), t + 1)
                if t >= 2:
                    dve.wait_ge(sem("mix_product"), t - 1)
                for k in range(4, 8):
                    ins = dve.tensor_scalar(mixT[:, t % 2, k, :], bank(1, P, at=P * (k - 4)), out_gain[:, k:k + 1], None, ALU.mult)
                    own(ins) if k < 7 else give(ins, "mixT_d")

            def moments(x, at=0):
                for c in range(2):
                    own(dve.bn_stats(bn[:, at + 6 * c:at + 6 * c + 6], x[:, 512 * c:512 * (c + 1)]))
                own(dve.bn_aggr(bn[:, at + 12:at + 14], bn[:, at:at + 12]))
                own(dve.tensor_scalar(bn[:, at + 13:at + 14], bn[:, at + 13:at + 14], EPS, None, ALU.add))
                rsqrt(bn[:, at + 14:at + 15], bn[:, at + 13:at + 14], bn[:, at + 15:at + 16])

            def first_norm(t):
                dve.wait_ge(sem("mix_product"), t + 1)
                b = 4 + 2 * (t % 2)
                own(tt(resid, PS[:, 512 * b:512 * (b + 2)], g1[int(t == NLAT)], ALU.mult))
                dve.wait_ge(sem(f"xres_loaded{t % 2}"), 16 * (t // 2 + 1))
                give(dve.scalar_tensor_tensor(resid, xres[:, t % 2, :], ALPHA, resid, ALU.mult, ALU.add), "resid_ready")
                if t:
                    dve.wait_ge(sem("h2_ready"), t)
                moments(resid)
                give(dve.tensor_scalar(xnorm, resid, bn[:, 12:13], bn[:, 14:15], ALU.subtract, ALU.mult), "xnorm_ready")

            def take_logits(t):
                dve.wait_ge(sem("logit_product"), t + 1)
                give(tt(logits[:, t, :], bank(2, ROUTE_W), route_bias, ALU.add), "logits_ready")

            dve.wait_ge(sem("g1_loaded"), 32)
            gain_half(0)
            for t in range(NTILE + 3):
                if t + 1 < NTILE:
                    gain_half(t + 1)
                if 1 <= t <= NTILE:
                    first_norm(t - 1)
                if t >= 3:
                    take_logits(t - 3)

            def first_largest(out, values, largest, eq, least, n):
                wide = [P, NTILE, n]
                own(tt(eq, values, largest.unsqueeze(2).broadcast_to(wide), ALU.is_equal))
                axpy(eq, eq, -64.0, row128[:, 0:n].unsqueeze(1).broadcast_to(wide))
                own(dve.tensor_reduce(least, eq, AX.X, ALU.min))
                own(tt(out, eq, least.unsqueeze(2).broadcast_to(wide), ALU.is_equal))

            groups = logits[:, :, 0:NGRP]
            experts = logits[:, :, NGRP:].rearrange("p t (g e) -> p t g e", g=NGRP)
            own(dve.tensor_reduce(r_max, groups, AX.X, ALU.max))
            give(tt(r_g, groups, r_max.unsqueeze(2).broadcast_to([P, NTILE, NGRP]), ALU.subtract), "group_shifted")
            dve.wait_ge(sem("group_exp"), 1)
            own(dve.tensor_reduce(r_pg, r_exp, AX.X, ALU.add))
            own(dve.reciprocal(r_pg, r_pg))
            first_largest(r_g, groups, r_max, r_eq, r_min, NGRP)
            own(tt(r_prod, experts, r_g.unsqueeze(3).broadcast_to([P, NTILE, NGRP, EPG]), ALU.mult))
            own(dve.tensor_reduce(r_sel, r_prod.rearrange("p t g e -> p t e g"), AX.X, ALU.add))
            for c in range(2):
                own(dve.tensor_reduce(r_v[:, c, :], r_sel, AX.X, ALU.max))
                first_largest(r_pick[:, c, :, :], r_sel, r_v[:, c, :], r_cand, r_min, EPG)
                if c == 0:
                    axpy(r_sel, r_pick[:, 0, :, :], -BIG, r_sel)
            give(tt(r_d, r_v[:, 1, :], r_v[:, 0, :], ALU.subtract), "pair_shifted")
            dve.wait_ge(sem("pair_exp"), 1)
            own(dve.tensor_scalar(r_max, r_d, 1.0, None, ALU.add))
            own(dve.reciprocal(r_max, r_max))
            own(tt(mix_w[:, 0, :], r_pg, r_max, ALU.mult))
            own(tt(mix_w[:, 1, :], mix_w[:, 0, :], r_d, ALU.mult))
            four = [P, NTILE, NGRP, EPG]
            for c in range(2):
                own(tt(r_mask[:, c, :, :].rearrange("p t (g e) -> p t g e", g=NGRP), r_g.unsqueeze(3).broadcast_to(four),
                       r_pick[:, c, :, :].unsqueeze(2).broadcast_to(four), ALU.mult))
            own(tt(r_all, r_mask[:, 0, :, :], r_mask[:, 1, :, :], ALU.add))
            own(dve.memset(r_before[:, 0, :], 0.0))
            for t in range(NTILE):
                ins = tt(r_before[:, t + 1, :], r_before[:, t, :], r_all[:, t, :], ALU.add)
                own(ins) if t + 1 < NTILE else give(ins, "assigned")
            dve.wait_ge(sem("rank_product"), 1)
            own(dve.tensor_copy(r_count, bank(1, NEXP)))
            own(dve.tensor_scalar(r_blocks, r_count, 0.0, None, ALU.is_gt))
            for m in range(1, NTILE):
                own(dve.scalar_tensor_tensor(r_blocks, r_count, float(P * m), r_blocks, ALU.is_gt, ALU.add))
            own(dve.tensor_copy(r_scan[:, 0, :], r_blocks))
            for i in range(5):
                src, dst, step = r_scan[:, i % 2, :], r_scan[:, (i + 1) % 2, :], 1 << i
                own(dve.tensor_copy(dst[:, 0:step], src[:, 0:step]))
                own(tt(dst[:, step:], src[:, step:], src[:, 0:NEXP - step], ALU.add))
            ends = r_scan[:, 1, :]
            blocks_first = [P, MAX_BLOCKS, NEXP]
            own(tt(r_cmp, ends.unsqueeze(1).broadcast_to(blocks_first),
                   row128[:, 0:MAX_BLOCKS].unsqueeze(2).broadcast_to(blocks_first), ALU.is_le))
            own(dve.tensor_reduce(r_eid[:, 0:MAX_BLOCKS], r_cmp, AX.X, ALU.add))
            own(dve.tensor_scalar(r_eid[:, 0:MAX_BLOCKS], r_eid[:, 0:MAX_BLOCKS], float(NEXP - 1), None, ALU.min))
            own(dve.tensor_copy(control[:, 0:MAX_BLOCKS], r_eid[0:1, 0:MAX_BLOCKS]))
            own(dve.tensor_scalar(r_eid[:, 60:61], ends[:, NEXP - 1:NEXP], 1.0, None, ALU.add))
            own(dve.tensor_copy(control[:, 61:62], r_eid[0:1, 60:61]))
            give(dve.tensor_scalar(control[:, 60:61], control[:, 61:62], 1, None, ALU.logical_shift_right), "control_ready")
            sub(r_base, ends, r_blocks)
            scaled(r_base, r_base, float(P))
            own(tt(r_slot, bank(0, NTILE * NEXP).rearrange("p (t n) -> p t n", t=NTILE),
                   r_base.unsqueeze(1).broadcast_to([P, NTILE, NEXP]), ALU.add))
            for c in range(2):
                own(tt(r_mask[:, c, :, :], r_mask[:, c, :, :], r_slot, ALU.mult))
                own(dve.tensor_reduce(r_pos[:, NTILE * c:NTILE * (c + 1)], r_mask[:, c, :, :], AX.X, ALU.add))
            own(dve.tensor_copy(slot_of, r_pos))
            n = 2 * NTILE
            own(dve.tensor_scalar(r_int[:, 0:n], slot_of, P - 1, None, ALU.bitwise_and))
            own(dve.tensor_scalar(r_int[:, n:2 * n], slot_of, 7, None, ALU.logical_shift_right))
            own(dve.tensor_copy(r_rowblk.rearrange("p a n -> p (a n)"), r_int))
            own(tt(r_hot, row128.unsqueeze(1).broadcast_to([P, n, P]), r_rowblk[:, 0, :].unsqueeze(2).broadcast_to([P, n, P]),
                   ALU.is_equal))
            blocks_last = [P, n, MAX_BLOCKS]
            own(tt(r_tok, row128[:, 0:MAX_BLOCKS].unsqueeze(1).broadcast_to(blocks_last),
                   r_rowblk[:, 1, :].unsqueeze(2).broadcast_to(blocks_last), ALU.is_equal))
            numbered = r_tok.rearrange("p (c t) n -> p c t n", c=2)
            give(tt(numbered, numbered, token_no[:, 0:NTILE].unsqueeze(1).unsqueeze(3).broadcast_to([P, 2, NTILE, MAX_BLOCKS]),
                    ALU.mult), "hot_ready")
            dve.wait_ge(sem("slot_product"), 1)
            give(dve.tensor_copy(slot_token, bank(4, MAX_BLOCKS)), "route_done")

            pairs = dve.value_load(control[0:1, 60:61], min_val=1, max_val=MAX_BLOCKS // 2)
            dve.sem_inc(sem("y_d"), 2)
            with dve.Fori(0, pairs) as i:
                for u in range(2):
                    dve.wait_ge(sem("x_transposed"), 2 * i + u + 3)
                    dve.tensor_copy(xgT[:, u, :, :], PS[:, 1024 * u:1024 * (u + 1)].rearrange("p (k n) -> p k n", k=KT)).then_inc(
                        sem("xT_ready"), 1)
                for u in range(2):
                    dve.wait_ge(sem("gate_ready"), 2 * i + u + 1)
                    tt(hT[:, u, :, :], gate_act[:, u, :, :], bank(4 + u, 256, at=256).rearrange("p (s n) -> p s n", s=2),
                       ALU.mult).then_inc(sem("hidden_ready"), 1)
                for u in range(2):
                    dve.wait_ge(sem("block_done"), 2 * i + u + 3)
                    dve.wait_ge(sem(f"slot_y_stored{u}"), 16 * i + 16)
                    dve.tensor_copy(ybuf[:, u, 512:1024], bank((7, 3)[u])).then_inc(sem("y_d"), 1)

            dve.wait_ge(sem("g2_loaded"), 32)
            for t in range(NTILE):
                a, at = acc[:, t % YN, :], 16 * (t % YN)
                dve.wait_ge(sem("first_weighted"), t + 1)
                give(dve.scalar_tensor_tensor(a, yg[:, t % YG, 1, :], mix_w[:, 1, t:t + 1], a, ALU.mult, ALU.add), "acc_ready")
                own(tt(a, a, g2[int(t == NLAT)], ALU.mult))
                axpy(a, x1[:, t, :], ALPHA, a)
                if t >= YN:
                    dve.wait_ge(sem("ynorm_ready"), t - YN + 1)
                moments(a, at)
                give(dve.scalar_tensor_tensor(bn[:, at + 15:at + 16], bn[:, at + 12:at + 13], -1.0, bn[:, at + 14:at + 15],
                                              ALU.mult, ALU.mult), "stats_ready")


def kernel(**inputs):
    import numpy as _np
    import concourse.bacc as _bacc
    from concourse import mybir as _mybir
    from concourse.bass_utils import run_bass_kernel_spmd as _run

    a = {k: _np.asarray(v) for k, v in inputs.items()}
    lay = _np.ascontiguousarray
    tok = _np.concatenate([a["x_sample"][0], a["x_prompt"][0]], 0)

    def columns(v):
        return v.reshape(-1, P).T

    cond = _np.stack([a["c"][0], a["c_ctx"]], 0).reshape(2, P, KT).transpose(1, 0, 2).reshape(P, 2 * KT)
    b_mod = a["b_mod"][0]
    arrays = {
        "cols": _np.concatenate([
            a["hy_short_w"][0].T.reshape(FEATS, P, 3).transpose(1, 0, 2).reshape(P, 3 * FEATS),
            columns(a["hy_short_b"][0]),
            columns(a["hy_skip"][0].reshape(-1)),
            columns(_np.concatenate([a["attn_out_gain"][0], a["hy_out_gain"][0]])),
            b_mod[0:D].reshape(P, KT), b_mod[D:2 * D].reshape(P, KT), cond], 1),
        "tables": small_tables(), "ntime": negative_times(), "feats": position_features(),
        "mats": fourier_matrices(), "rot": rotary_tables(),
        "hid": _np.concatenate([a["hy_f_w2"][0], a["hy_f_b1"][0][:, None], a["hy_f_b2"][0][:, None], a["hy_freq"][0][:, None]], 1),
        "hy_f_w1": a["hy_f_w1"][0], "hy_f_w3": a["hy_f_w3"][0], "hy_decay": a["hy_decay"][0],
        "qk_gain": _np.concatenate([a["q_gain"][0]] * HEADS + [a["k_gain"][0]] * KV),
        "route_bias": _np.concatenate([a["router_grp_b"][0], a["router_exp_b"][0]]),
        "route_w": _np.concatenate([a["router_grp_w"][0], a["router_exp_w"][0]], 1),
        "w_mod": a["w_mod"][0], "b_mod": b_mod, "w_in": a["w_in"][0], "w_out": a["w_out"][0],
        "xT": tok.T, "x_tok": tok,
        "cache_k": a["cache_k"][0, 0].reshape(P, KV * HD), "cache_v": a["cache_v"][0, 0].reshape(P, KV * HD),
        "ln1_g": a["ln1_g"][0], "ln1_b": a["ln1_b"][0], "ln2_g": a["ln2_g"][0], "ln2_b": a["ln2_b"][0],
        "exp_w_gate": a["exp_w_gate"][0], "exp_w_up": a["exp_w_up"][0], "exp_w_down": a["exp_w_down"][0],
    }
    arrays = {k: lay(v) for k, v in arrays.items()}
    nc = _bacc.Bacc("TRN2", target_bir_lowering=False, num_devices=1)
    I = {k: nc.dram_tensor("in_" + k, list(v.shape), _mybir.dt.from_np(v.dtype), kind="ExternalInput").ap()
         for k, v in arrays.items()}
    shapes = {"ctx": [CTX, D], "lat": [LAT, D], "new_k": [CTX, KV * HD], "new_v": [CTX, KV * HD]}
    O = {k: nc.dram_tensor("out_" + k, s, F32, kind="ExternalOutput").ap() for k, s in shapes.items()}
    build(nc, I, O)
    r = _run(nc, [{"in_" + k: v for k, v in arrays.items()}], core_ids=[0]).results[0]
    cache = (1, 1, CTX, KV, HD)
    return (r["out_ctx"].reshape(1, CTX, D), r["out_lat"].reshape(1, LAT, D),
            r["out_new_k"].reshape(cache), r["out_new_v"].reshape(cache))
```
